# Optimizing a Trainium2 kernel written in Bass

```python
import jax, jax.numpy as jnp
from jax import lax
import numpy as np

D_MODEL = 1024
BATCH = 1
SEQ = 2048
DEPTH = 1
DEC_BATCH = 8
DEC_SEQ = 8
PAST_LEN = 8192
PAGE_SIZE = 128

A_HEADS = 8
A_HEAD_DIM = 64
D_A = A_HEADS * A_HEAD_DIM
Q_BLOCK = 128
FORGET_BIAS = 3.0
B_HEADS = 4
B_KEY_DIM = 64
B_VAL_DIM = 128
D_BK = B_HEADS * B_KEY_DIM
D_B = B_HEADS * B_VAL_DIM
GLA_LOW_RANK = 16
GLA_TAU = 16.0
GLA_CHUNK = 64
D_C = D_MODEL // 2
CONV_W = 3

N_BRANCH = 3
EPS = 1e-6
SPLIT_SIZES = (D_A, D_A, D_A, A_HEADS, D_A,
               D_BK, D_BK, D_B, GLA_LOW_RANK, D_B,
               D_C, D_C, D_C, D_C,
               N_BRANCH * D_MODEL)
N_IN = sum(SPLIT_SIZES)

kernel_name = 'hybrid_fox_gla_shortconv_decode_step'

def rms_norm(x, g):
    xf = x.astype(jnp.float32)
    y = xf * lax.rsqrt(jnp.mean(xf * xf, axis=-1, keepdims=True) + EPS) * g.astype(jnp.float32)
    return y.astype(x.dtype)

def split_columns(z):
    idx = [int(i) for i in np.cumsum(SPLIT_SIZES)[:-1]]
    return jnp.split(z, idx, axis=-1)

def fox_attention(q, k, v, fq, fk, q_pos, k_pos):
    bsz, tq, h, dh = q.shape
    blk = min(Q_BLOCK, tq)
    nb = -(-tq // blk)
    pad = nb * blk - tq
    qp = jnp.pad(q, ((0, 0), (0, pad), (0, 0), (0, 0)))
    fqp = jnp.pad(fq, ((0, 0), (0, pad), (0, 0)))
    posp = jnp.pad(q_pos, (0, pad), mode='edge')
    qb = qp.reshape(bsz, nb, blk, h, dh).transpose(1, 0, 2, 3, 4)
    fqb = fqp.reshape(bsz, nb, blk, h).transpose(1, 0, 2, 3)
    pb = posp.reshape(nb, blk)
    fk_t = fk.transpose(0, 2, 1)
    scale = dh ** -0.5

    def one_block(args):
        qi, fi, pi = args
        s = jnp.einsum('bqhd,bkhd->bhqk', qi, k, preferred_element_type=jnp.float32) * scale
        s = s + fi.transpose(0, 2, 1)[..., :, None] - fk_t[..., None, :]
        mask = k_pos[None, :] <= pi[:, None]
        s = jnp.where(mask, s, -jnp.inf)
        p = jax.nn.softmax(s, axis=-1)
        return jnp.einsum('bhqk,bkhd->bqhd', p.astype(v.dtype), v)

    out = lax.map(one_block, (qb, fqb, pb))
    return out.transpose(1, 0, 2, 3, 4).reshape(bsz, nb * blk, h, dh)[:, :tq]

def gla_chunked(q, k, v, log_a, s0):
    bsz, t, h, dk = q.shape
    dv = v.shape[-1]
    c = min(GLA_CHUNK, t)
    n = -(-t // c)
    pad = n * c - t

    def to_chunks(a):
        a = jnp.pad(a.astype(jnp.float32), ((0, 0), (0, pad), (0, 0), (0, 0)))
        return a.reshape(bsz, n, c, h, a.shape[-1]).transpose(1, 0, 3, 2, 4)

    qc = to_chunks(q * (dk ** -0.5))
    kc = to_chunks(k)
    vc = to_chunks(v)
    ac = to_chunks(log_a)
    causal = jnp.tril(jnp.ones((c, c), dtype=bool))

    def step(state, inp):
        qi, ki, vi, ai = inp
        b = jnp.cumsum(ai, axis=2)
        o_inter = jnp.einsum('bhtd,bhde->bhte', qi * jnp.exp(b), state)
        diff = b[:, :, :, None, :] - b[:, :, None, :, :]
        decay = jnp.exp(jnp.where(causal[:, :, None], diff, -jnp.inf))
        att = jnp.einsum('bhtd,bhsd,bhtsd->bhts', qi, ki, decay)
        o = o_inter + jnp.einsum('bhts,bhse->bhte', att, vi)
        b_last = b[:, :, -1:, :]
        new_state = (jnp.exp(b_last[:, :, 0, :])[..., None] * state
                     + jnp.einsum('bhsd,bhse->bhde', ki * jnp.exp(b_last - b), vi))
        return new_state, o

    s_final, oc = lax.scan(step, s0.astype(jnp.float32), (qc, kc, vc, ac))
    o = oc.transpose(1, 0, 3, 2, 4).reshape(bsz, n * c, h, dv)[:, :t]
    return o, s_final

def short_conv(u, buf, w):
    t = u.shape[1]
    ext = jnp.concatenate([buf.astype(u.dtype), u], axis=1)
    y = w[0] * ext[:, 0:t]
    for i in range(1, CONV_W):
        y = y + w[i] * ext[:, i:i + t]
    return y, ext[:, -(CONV_W - 1):]

def hybrid_layer(x, kv_past, gla_state, conv_state, g_norm, w_in, b_forget, w_gla_up, b_gla,
                 g_gla, conv_w, w_branch_a, w_branch_b, w_branch_c, w_out):
    bsz, t, _ = x.shape
    h = rms_norm(x, g_norm)
    z = jnp.einsum('btd,dn->btn', h, w_in)
    (qa, ka, va, fa, ga, qb, kb, vb, lrb, gb, xc, bc, cc, gc, mg) = split_columns(z)

    qa = qa.reshape(bsz, t, A_HEADS, A_HEAD_DIM)
    ka = ka.reshape(bsz, t, A_HEADS, A_HEAD_DIM)
    va = va.reshape(bsz, t, A_HEADS, A_HEAD_DIM)
    logf = jax.nn.log_sigmoid(fa.astype(jnp.float32) + b_forget.astype(jnp.float32))
    if kv_past is None:
        offset = 0
        k_all, v_all, logf_all = ka, va, logf
    else:
        k_past, v_past, logf_past = kv_past
        offset = k_past.shape[1]
        k_all = jnp.concatenate([k_past.astype(ka.dtype), ka], axis=1)
        v_all = jnp.concatenate([v_past.astype(va.dtype), va], axis=1)
        logf_all = jnp.concatenate([logf_past.astype(jnp.float32), logf], axis=1)
    cum_f = jnp.cumsum(logf_all, axis=1)
    q_pos = offset + jnp.arange(t)
    k_pos = jnp.arange(offset + t)
    ya = fox_attention(qa, k_all, v_all, cum_f[:, offset:], cum_f, q_pos, k_pos)
    ya = ya.reshape(bsz, t, D_A) * jax.nn.silu(ga)

    qb = qb.reshape(bsz, t, B_HEADS, B_KEY_DIM)
    kb = kb.reshape(bsz, t, B_HEADS, B_KEY_DIM)
    vb = vb.reshape(bsz, t, B_HEADS, B_VAL_DIM)
    a_logit = jnp.einsum('btr,rk->btk', lrb, w_gla_up) + b_gla
    log_a = (jax.nn.log_sigmoid(a_logit.astype(jnp.float32)) / GLA_TAU).reshape(bsz, t, B_HEADS, B_KEY_DIM)
    ob, gla_new = gla_chunked(qb, kb, vb, log_a, gla_state)
    ob = rms_norm(ob, g_gla.reshape(B_HEADS, B_VAL_DIM)).astype(x.dtype)
    yb = ob.reshape(bsz, t, D_B) * jax.nn.silu(gb)

    u = cc * xc
    yconv, conv_new = short_conv(u, conv_state, conv_w)
    yc = bc * yconv * jax.nn.silu(gc)

    gates = jax.nn.sigmoid(mg.astype(jnp.float32)).astype(x.dtype).reshape(bsz, t, N_BRANCH, D_MODEL)
    merged = (gates[:, :, 0] * jnp.einsum('bte,ed->btd', ya, w_branch_a)
              + gates[:, :, 1] * jnp.einsum('bte,ed->btd', yb, w_branch_b)
              + gates[:, :, 2] * jnp.einsum('bte,ed->btd', yc, w_branch_c))
    out = x + jnp.einsum('btd,de->bte', merged, w_out)
    return out, ka, va, logf, gla_new, conv_new

def setup_inputs(seed: int = 0) -> dict:
    key = jax.random.key(seed)
    ks = jax.random.split(key, 24)
    f32 = jnp.float32
    n_pages = PAST_LEN // PAGE_SIZE
    n_used = DEC_BATCH * n_pages
    n_pool = (n_used * 5) // 4

    def nrm(k, shape, s):
        return jax.random.normal(k, shape, f32) * s

    x_prompt = nrm(ks[0], (BATCH, SEQ, D_MODEL), 1.0)
    x_sample = nrm(ks[1], (DEC_BATCH, DEC_SEQ, D_MODEL), 1.0)
    cache_k = nrm(ks[2], (DEPTH, n_pool, PAGE_SIZE, A_HEADS, A_HEAD_DIM), 1.0)
    cache_v = nrm(ks[3], (DEPTH, n_pool, PAGE_SIZE, A_HEADS, A_HEAD_DIM), 1.0)
    cache_logf = jax.nn.log_sigmoid(FORGET_BIAS + nrm(ks[4], (DEPTH, n_pool, PAGE_SIZE, A_HEADS), 1.0))
    state_gla = nrm(ks[5], (DEPTH, DEC_BATCH, B_HEADS, B_KEY_DIM, B_VAL_DIM), 0.5)
    state_conv = nrm(ks[6], (DEPTH, DEC_BATCH, CONV_W - 1, D_C), 1.0)
    page_table = jax.random.permutation(ks[7], n_pool)[:n_used].reshape(DEC_BATCH, n_pages).astype(jnp.int32)
    g_norm = 1.0 + nrm(ks[8], (DEPTH, D_MODEL), 0.05)
    w_in = nrm(ks[9], (DEPTH, D_MODEL, N_IN), D_MODEL ** -0.5)
    b_forget = FORGET_BIAS + nrm(ks[10], (DEPTH, A_HEADS), 0.1)
    w_gla_up = nrm(ks[11], (DEPTH, GLA_LOW_RANK, D_BK), GLA_LOW_RANK ** -0.5)
    b_gla = nrm(ks[12], (DEPTH, D_BK), 0.01)
    g_gla = 1.0 + nrm(ks[13], (DEPTH, D_B), 0.05)
    conv_w = nrm(ks[14], (DEPTH, CONV_W, D_C), CONV_W ** -0.5)
    w_branch_a = nrm(ks[15], (DEPTH, D_A, D_MODEL), D_A ** -0.5)
    w_branch_b = nrm(ks[16], (DEPTH, D_B, D_MODEL), D_B ** -0.5)
    w_branch_c = nrm(ks[17], (DEPTH, D_C, D_MODEL), D_C ** -0.5)
    w_out = nrm(ks[18], (DEPTH, D_MODEL, D_MODEL), D_MODEL ** -0.5)
    g_final = 1.0 + nrm(ks[19], (D_MODEL,), 0.05)
    return {'x_prompt': x_prompt, 'x_sample': x_sample,
            'cache_k': cache_k, 'cache_v': cache_v, 'cache_logf': cache_logf,
            'state_gla': state_gla, 'state_conv': state_conv, 'page_table': page_table,
            'g_norm': g_norm, 'w_in': w_in, 'b_forget': b_forget, 'w_gla_up': w_gla_up,
            'b_gla': b_gla, 'g_gla': g_gla, 'conv_w': conv_w, 'w_branch_a': w_branch_a,
            'w_branch_b': w_branch_b, 'w_branch_c': w_branch_c, 'w_out': w_out, 'g_final': g_final}

def reference(x_prompt, x_sample, cache_k, cache_v, cache_logf, state_gla, state_conv, page_table,
              g_norm, w_in, b_forget, w_gla_up, b_gla, g_gla, conv_w, w_branch_a, w_branch_b,
              w_branch_c, w_out, g_final):
    n_pages = page_table.shape[1]
    past_len = n_pages * PAGE_SIZE
    bp = x_prompt.shape[0]
    bs = x_sample.shape[0]
    xp, xs = x_prompt, x_sample
    kp_l, vp_l, fp_l, ks_l, vs_l, fs_l = [], [], [], [], [], []
    gp_l, gs_l, cp_l, cs_l = [], [], [], []
    for l in range(DEPTH):
        lw = (g_norm[l], w_in[l], b_forget[l], w_gla_up[l], b_gla[l], g_gla[l], conv_w[l],
              w_branch_a[l], w_branch_b[l], w_branch_c[l], w_out[l])
        gla0 = jnp.zeros((bp, B_HEADS, B_KEY_DIM, B_VAL_DIM), jnp.float32)
        conv0 = jnp.zeros((bp, CONV_W - 1, D_C), xp.dtype)
        xp, kp, vp, fp, gp, cp = hybrid_layer(xp, None, gla0, conv0, *lw)
        k_past = cache_k[l][page_table].reshape(bs, past_len, A_HEADS, A_HEAD_DIM)
        v_past = cache_v[l][page_table].reshape(bs, past_len, A_HEADS, A_HEAD_DIM)
        f_past = cache_logf[l][page_table].reshape(bs, past_len, A_HEADS)
        xs, ksn, vsn, fsn, gsn, csn = hybrid_layer(xs, (k_past, v_past, f_past), state_gla[l], state_conv[l], *lw)
        kp_l.append(kp); vp_l.append(vp); fp_l.append(fp)
        ks_l.append(ksn); vs_l.append(vsn); fs_l.append(fsn)
        gp_l.append(gp); gs_l.append(gsn); cp_l.append(cp); cs_l.append(csn)
    y_prompt = rms_norm(xp, g_final)
    y_sample = rms_norm(xs, g_final)
    return (y_prompt, y_sample,
            jnp.stack(kp_l), jnp.stack(vp_l), jnp.stack(fp_l),
            jnp.stack(ks_l), jnp.stack(vs_l), jnp.stack(fs_l),
            jnp.stack(gp_l), jnp.stack(gs_l),
            jnp.stack(cp_l), jnp.stack(cs_l))


_drawn_inputs = setup_inputs


def setup_inputs(seed=0):
    import zlib

    import numpy as np

    out = dict(_drawn_inputs(seed))
    spreads = {}
    factors = {'cache_logf': 5.088, 'b_gla': 8.0, 'g_gla': 3.897}
    for name, (base, spread) in spreads.items():
        noise = np.random.default_rng([zlib.crc32(name.encode()), seed]).standard_normal(out[name].shape)
        drawn = base * np.exp(spread * noise) if base else spread * noise
        out[name] = __import__('jax').numpy.asarray(drawn.astype(out[name].dtype))
    for name, factor in factors.items():
        out[name] = (out[name] * factor).astype(out[name].dtype)
    return out
```

```python
from contextlib import ExitStack

import concourse.bass as bass
from concourse import mybir
from concourse.alu_op_type import AluOpType as ALU

ACT = mybir.ActivationFunctionType
AX = mybir.AxisListType
F32 = mybir.dt.float32
F32R = mybir.dt.float32r
BF16 = mybir.dt.bfloat16
I32 = mybir.dt.int32

P = 128
D_MODEL = 1024
KC = D_MODEL // P
SEQ, DEC_BATCH, DEC_SEQ = 2048, 8, 8
PAST_LEN, PAGE = 8192, 128
N_PAGES = PAST_LEN // PAGE
CHUNK_PAGES = 4
CHUNKS = N_PAGES // CHUNK_PAGES
HEADS, HEAD_DIM = 8, 64
D_A = HEADS * HEAD_DIM
B_HEADS, B_KEY, B_VAL = 4, 64, 128
D_BK, D_B = B_HEADS * B_KEY, B_HEADS * B_VAL
LOW_RANK, GLA_TAU = 16, 16.0
D_C = D_MODEL // 2
CONV_W = 3
EPS = 1e-6
SAMPLE = DEC_BATCH * DEC_SEQ
PROMPT_TILES = SEQ // P
TILES = PROMPT_TILES + 1
ROWS = TILES * P
BLK = 512
Z_QA, Z_KA, Z_VA, Z_GA, Z_QKB, Z_VB, Z_GB, Z_XC, Z_BC, Z_CC, Z_GC, Z_MG = range(12)
N_BLOCKS = Z_MG + 3 * D_MODEL // BLK
TABLES = "natural_log_exp_and_others"
TAIL = HEADS + LOW_RANK


class Pool:

    def __init__(self, nc, stack, phase):
        self.nc, self.stack, self.phase = nc, stack, phase
        self.used = []
        stack.callback(self.clear)

    def clear(self):
        self.nc.clear_and_free_semaphores(self.used)
        self.nc.all_engine_barrier()

    def sb(self, name, shape, dt=F32):
        return self.stack.enter_context(self.nc.sbuf_tensor(f"{self.phase}_{name}", shape, dt))

    def ps(self, name, shape, dt=F32):
        return self.stack.enter_context(self.nc.psum_tensor(f"{self.phase}_{name}", shape, dt))

    def sem(self, name):
        self.used.append(self.nc.alloc_semaphore(f"{self.phase}_{name}"))
        return self.used[-1]

    def sems(self, name, n):
        return [self.sem(f"{name}{i}") for i in range(n)]


def make_identity(pool, ident, zeroed, ready):
    pool.memset(ident[:], 0.0).then_inc(zeroed, 1)
    pool.wait_ge(zeroed, 1)
    pool.affine_select(out=ident[:], in_=ident[:], compare_op=ALU.not_equal, fill=1.0, base=0,
                       pattern=[[-1, P]], channel_multiplier=1).then_inc(ready, 1)


def project(nc, x_all, g_norm, w_main, w_tail, z, tail):
    GROUPS = [range(0, 9), range(9, TILES)]
    HT = len(GROUPS[0])
    RING = 4
    w_view = w_main.rearrange("(k p) (b n) -> b p k n", p=P, n=BLK)
    tail_view = w_tail.rearrange("(k p) n -> p k n", p=P)
    with ExitStack() as stack:
        m = Pool(nc, stack, "prj")
        ident = m.sb("ident", [P, P])
        gain = m.sb("gain", [P, D_MODEL])
        x_in = m.sb("x_in", [P, 2, D_MODEL])
        x_norm = m.sb("x_norm", [P, 2, D_MODEL])
        sumsq = m.sb("sumsq", [P, TILES])
        log_ms = m.sb("log_ms", [P, TILES])
        rstd = m.sb("rstd", [P, TILES])
        eps = m.sb("eps", [P, 1])
        h_hi = m.sb("h_hi", [P, HT, KC, P], F32R)
        h_lo = m.sb("h_lo", [P, HT, KC, P], F32R)
        w_raw = m.sb("w_raw", [P, 2, KC, BLK])
        w_hi = m.sb("w_hi", [P, 2, KC, BLK], F32R)
        w_lo = m.sb("w_lo", [P, 2, KC, BLK], F32R)
        z_sb = m.sb("z_sb", [P, RING, BLK])
        z_ps = m.ps("z_ps", [P, RING, BLK])
        t_ps = m.ps("t_ps", [P, 2, 2, BLK])

        zeroed, ident_ready = m.sem("zeroed"), m.sem("ident_ready")
        const_ready = m.sem("const_ready")
        x_loaded = m.sems("x_loaded", 2)
        squared = m.sem("squared")
        logged, rstd_ready = m.sem("logged"), m.sem("rstd_ready")
        x_ready = m.sem("x_ready")
        turned = m.sem("turned")
        hi_ready, lo_ready = m.sem("hi_ready"), m.sem("lo_ready")
        w_loaded = m.sems("w_loaded", 2)
        whi_ready, wlo_ready = m.sem("whi_ready"), m.sem("wlo_ready")
        z_done = m.sem("z_done")
        z_ready = m.sems("z_ready", RING)
        z_stored = m.sems("z_stored", RING)
        block = stack.enter_context(nc.Block())

        def uses(tiles, slot):
            return len(range(slot, len(tiles), RING))

        BLOCKS = N_BLOCKS + 1

        def each_block(eng, step):
            with eng.Fori(0, N_BLOCKS // 2) as j:
                step(j * 2, 0)
                step(j * 2 + 1, 1)
            step(N_BLOCKS - 1, 0)
            step(N_BLOCKS, 1)

        def width(i):
            return TAIL if isinstance(i, int) and i == N_BLOCKS else BLK

        @block.gpsimd
        def _(pool):
            make_identity(pool, ident, zeroed, ident_ready)
            pool.memset(eps[:], EPS).then_inc(const_ready, 16)

        @block.sync
        def _(sp):
            sp.dma_start(gain[:], g_norm.rearrange("l n -> (l n)").partition_broadcast(P)).then_inc(const_ready, 16)

            def load_weights(g, i, par):
                src = tail_view if isinstance(i, int) and i == N_BLOCKS else w_view[bass.ds(i, 1)].rearrange("b p k n -> (b p) k n")
                sp.dma_start(w_raw[:, par, :, 0:width(i)], src).then_inc(w_loaded[par], 16)

            for g, tiles in enumerate(GROUPS):
                for t in tiles:
                    if t >= 2:
                        sp.wait_ge(x_ready, t - 1)
                    sp.dma_start(x_in[:, t % 2], x_all[t * P:(t + 1) * P, :]).then_inc(x_loaded[t % 2], 16)
                    if t == tiles[0]:
                        if g > 0:
                            sp.wait_ge(whi_ready, g * BLOCKS)
                            sp.wait_ge(wlo_ready, g * BLOCKS)
                        load_weights(g, 0, 0)
                        load_weights(g, 1, 1)

                def step(i, par, g=g, tiles=tiles, base=g * BLOCKS):
                    if not (isinstance(i, int) and i >= N_BLOCKS - 1):
                        sp.wait_ge(whi_ready, i + (base + 1))
                        sp.wait_ge(wlo_ready, i + (base + 1))
                        load_weights(g, i + 2, par)
                    for n, t in enumerate(tiles):
                        slot, per = n % RING, uses(tiles, n % RING)
                        before = sum(BLOCKS * uses(x, slot) for x in GROUPS[:g])
                        sp.wait_ge(z_ready[slot], i * per + (before + n // RING + 1))
                        rows = slice(t * P, (t + 1) * P)
                        dst = tail[rows, :] if width(i) == TAIL else \
                            z[bass.ds(i, 1), rows, :].rearrange("b p n -> (b p) n")
                        sp.dma_start(dst, z_sb[:, slot, 0:width(i)]).then_inc(z_stored[slot], 16)

                with sp.Fori(0, N_BLOCKS // 2 - 1) as j:
                    step(j * 2, 0)
                    step(j * 2 + 1, 1)
                for i in range(N_BLOCKS - 3, N_BLOCKS + 1):
                    step(i, i % 2)
            for slot in range(RING):
                sp.wait_ge(z_stored[slot], 16 * BLOCKS * sum(uses(x, slot) for x in GROUPS))

        @block.scalar
        def _(act):
            act.preload_act_table_set(TABLES)
            act.wait_ge(const_ready, 32)
            for g, tiles in enumerate(GROUPS):
                base = g * BLOCKS

                done = sum(BLOCKS * len(x) for x in GROUPS[:g])

                def split(i, par, base=base):
                    act.wait_ge(w_loaded[par], (i - par) * 8 + 8 * (base + 2))
                    act.copy(w_hi[:, par, :, 0:width(i)], w_raw[:, par, :, 0:width(i)]).then_inc(whi_ready, 1)

                for n, t in enumerate(tiles):
                    act.wait_ge(x_loaded[t % 2], 16 * (t // 2 + 1))
                    if t >= 2:
                        act.wait_ge(turned, t - 1)
                    act.activation(x_norm[:, t % 2], x_in[:, t % 2], ACT.Square, accum_out=sumsq[:, t:t + 1]).then_inc(squared, 1)
                    act.wait_ge(squared, t + 1)
                    act.activation(log_ms[:, t:t + 1], sumsq[:, t:t + 1], ACT.Ln, bias=eps[:, 0:1], scale=1.0 / D_MODEL).then_inc(logged, 1)
                    act.wait_ge(logged, t + 1)
                    act.activation(rstd[:, t:t + 1], log_ms[:, t:t + 1], ACT.Exp, scale=-0.5).then_inc(rstd_ready, 1)
                    act.wait_ge(turned, t + 1)
                    if g > 0:
                        act.wait_ge(z_done, done)
                    act.copy(h_hi[:, n], t_ps[:, t % 2].rearrange("p a (b c) -> p (a b) c", c=P)).then_inc(hi_ready, 1)
                split(0, 0)

                def step(i, par, g=g, tiles=tiles, done=done):
                    if not (isinstance(i, int) and i == N_BLOCKS):
                        act.wait_ge(z_done, i * len(tiles) + done)
                        split(i + 1, 1 - par)
                    for n in range(len(tiles)):
                        slot, per = n % RING, uses(tiles, n % RING)
                        before = sum(BLOCKS * uses(x, slot) for x in GROUPS[:g])
                        act.wait_ge(z_done, i * len(tiles) + (done + n + 1))
                        act.wait_ge(z_stored[slot], (i * per + (before + n // RING)) * 16)
                        act.copy(z_sb[:, slot, 0:width(i)], z_ps[:, slot, 0:width(i)]).then_inc(z_ready[slot], 1)

                each_block(act, step)

        @block.vector
        def _(dve):
            dve.wait_ge(const_ready, 32)
            for g, tiles in enumerate(GROUPS):
                base = g * BLOCKS
                for n, t in enumerate(tiles):
                    dve.wait_ge(rstd_ready, t + 1)
                    dve.scalar_tensor_tensor(out=x_norm[:, t % 2], in0=x_in[:, t % 2], scalar=rstd[:, t:t + 1],
                                             in1=gain[:], op0=ALU.mult, op1=ALU.mult).then_inc(x_ready, 1)
                    dve.wait_ge(hi_ready, t + 1)
                    dve.tensor_tensor(h_lo[:, n], t_ps[:, t % 2].rearrange("p a (b c) -> p (a b) c", c=P),
                                      h_hi[:, n].bitcast(F32), ALU.subtract).then_inc(lo_ready, 1)

                def step(i, par, base=base):
                    dve.wait_ge(whi_ready, i + (base + 1))
                    dve.tensor_tensor(w_lo[:, par, :, 0:width(i)], w_raw[:, par, :, 0:width(i)],
                                      w_hi[:, par, :, 0:width(i)].bitcast(F32), ALU.subtract).then_inc(wlo_ready, 1)

                each_block(dve, step)

        @block.tensor
        def _(pe):
            pe.wait_ge(ident_ready, 1)
            for g, tiles in enumerate(GROUPS):
                base = g * BLOCKS
                for n, t in enumerate(tiles):
                    pe.wait_ge(x_ready, t + 1)
                    if t >= 2:
                        pe.wait_ge(lo_ready, t - 1)
                    for k in range(KC):
                        last = pe.transpose(t_ps[:, t % 2, k // 4, (k % 4) * P:(k % 4 + 1) * P],
                                            x_norm[:, t % 2, k * P:(k + 1) * P], ident[:])
                    last.then_inc(turned, 1)
                pe.wait_ge(lo_ready, tiles[-1] + 1)

                def step(i, par, g=g, tiles=tiles, base=base):
                    pe.wait_ge(wlo_ready, i + (base + 1))
                    w = width(i)
                    for n in range(len(tiles)):
                        slot, per = n % RING, uses(tiles, n % RING)
                        before = sum(BLOCKS * uses(x, slot) for x in GROUPS[:g])
                        pe.wait_ge(z_ready[slot], i * per + (before + n // RING))
                        terms = [(a, b, k) for k in range(KC) for a, b in ((h_hi, w_hi), (h_hi, w_lo), (h_lo, w_hi))]
                        for q, (a, b, k) in enumerate(terms):
                            mm = pe.matmul(z_ps[:, slot, 0:w], a[:, n, k, :], b[:, par, k, 0:w],
                                           start=(q == 0), stop=(q == len(terms) - 1))
                        mm.then_inc(z_done, 1)

                each_block(pe, step)


def forget_gates(nc, tail, b_forget, logf, decay_key, logf_prompt, logf_sample):
    with ExitStack() as stack:
        m = Pool(nc, stack, "fg")
        N = TILES * HEADS
        NP = PROMPT_TILES * HEADS
        logits = m.sb("logits", [P, TILES, HEADS])
        bias = m.sb("bias", [P, HEADS])
        x = m.sb("x", [P, TILES, HEADS])
        mag = m.sb("mag", [P, N])
        e = m.sb("e", [P, N])
        soft = m.sb("soft", [P, N])
        low = m.sb("low", [P, N])
        lf = m.sb("lf", [P, TILES, HEADS])
        before = m.sb("before", [P, TILES, HEADS])
        ones = m.sb("ones", [P, P])
        upto = m.sb("upto", [P, P])
        neg = m.sb("neg", [P, NP])
        hi = m.sb("hi", [P, NP], F32R)
        lo = m.sb("lo", [P, NP])
        cum = m.ps("cum", [P, BLK])
        loaded, consts, v, s = m.sem("loaded"), m.sem("consts"), m.sem("vector_step"), m.sem("scalar_step")
        summed, stored = m.sem("summed"), m.sem("stored")
        block = stack.enter_context(nc.Block())

        @block.sync
        def _(sp):
            sp.dma_start(logits[:], tail.rearrange("(t p) c -> p t c", p=P)[:, :, 0:HEADS]).then_inc(loaded, 16)
            sp.dma_start(bias[:], b_forget.rearrange("l n -> (l n)").partition_broadcast(P)).then_inc(loaded, 16)
            sp.wait_ge(v, 3)
            sp.dma_start(logf.rearrange("(t p) h -> p t h", p=P), lf[:]).then_inc(stored, 16)
            sp.dma_start(logf_prompt.rearrange("l b (t p) h -> p (l b t) h", p=P), lf[:, 0:PROMPT_TILES]).then_inc(stored, 16)
            sp.dma_start(logf_sample.rearrange("l b s h -> (l b s) h"), lf[0:SAMPLE, PROMPT_TILES]).then_inc(stored, 16)
            sp.wait_ge(v, 6 + HEADS)
            for part, src in enumerate((hi[:].bitcast(F32), lo[:])):
                sp.dma_start(decay_key[part], src).then_inc(stored, 16)
            sp.wait_ge(stored, 16 * 5)

        @block.gpsimd
        def _(pool):
            pool.memset(ones[:], 1.0).then_inc(consts, 1)
            pool.wait_ge(consts, 1)
            pool.affine_select(out=upto[:], in_=ones[:], compare_op=ALU.is_ge, fill=0.0, base=0,
                               pattern=[[1, P]], channel_multiplier=-1).then_inc(consts, 1)

        @block.scalar
        def _(act):
            act.preload_act_table_set(TABLES)
            act.wait_ge(v, 1)
            act.activation(mag[:], x[:].rearrange("p t h -> p (t h)"), ACT.Abs).then_inc(s, 1)
            act.wait_ge(s, 1)
            act.activation(e[:], mag[:], ACT.Exp, scale=-1.0).then_inc(s, 1)
            act.wait_ge(s, 2)
            act.activation(soft[:], e[:], ACT.Ln, bias=1.0).then_inc(s, 1)

        @block.vector
        def _(dve):
            dve.wait_ge(loaded, 32)
            dve.tensor_tensor(x[:], logits[:], bias[:].unsqueeze(1).broadcast_to([P, TILES, HEADS]), ALU.add).then_inc(v, 1)
            dve.wait_ge(v, 1)
            dve.tensor_scalar(low[:], x[:].rearrange("p t h -> p (t h)"), 0.0, None, ALU.min).then_inc(v, 1)
            dve.wait_ge(v, 2)
            dve.wait_ge(s, 3)
            dve.tensor_tensor(lf[:].rearrange("p t h -> p (t h)"), low[:], soft[:], ALU.subtract).then_inc(v, 1)
            dve.wait_ge(v, 3)
            dve.memset(before[:, 0], 0.0)
            for h in range(HEADS):
                dve.tensor_tensor_scan(before[:, 1:PROMPT_TILES, h], lf[:, 0:PROMPT_TILES - 1, h],
                                       lf[:, 0:PROMPT_TILES - 1, h], 0.0, ALU.add, ALU.bypass).then_inc(v, 1)
            dve.wait_ge(summed, 1)
            dve.tensor_scalar(neg[:], cum[:, 0:NP], -1.0, None, ALU.mult).then_inc(v, 1)
            dve.wait_ge(v, 4 + HEADS)
            dve.tensor_copy(hi[:], neg[:]).then_inc(v, 1)
            dve.wait_ge(v, 5 + HEADS)
            dve.tensor_tensor(lo[:], neg[:], hi[:].bitcast(F32), ALU.subtract).then_inc(v, 1)

        @block.tensor
        def _(pe):
            pe.wait_ge(consts, 2)
            pe.wait_ge(v, 3 + HEADS)
            flat = lf[:].rearrange("p t h -> p (t h)")
            pe.matmul(cum[:, 0:NP], upto[:], flat[:, 0:NP], start=True, stop=False)
            pe.matmul(cum[:, 0:NP], ones[:], before[:].rearrange("p t h -> p (t h)")[:, 0:NP], start=False,
                      stop=True).then_inc(summed, 1)


def gla_decay(nc, tail, w_up, b_gla, gla_cum):
    PAIRS = B_HEADS // 2
    COLS = [(c, min(BLK, ROWS - c)) for c in range(0, ROWS, BLK)]
    with ExitStack() as stack:
        m = Pool(nc, stack, "gd")
        low = m.sb("low", [P, TILES, LOW_RANK])
        lowT = m.sb("lowT", [LOW_RANK, ROWS])
        up = m.sb("up", [LOW_RANK, D_BK])
        bias = m.sb("bias", [P, PAIRS])
        x = m.sb("x", [P, PAIRS, ROWS])
        mag = m.sb("mag", [P, PAIRS, ROWS])
        soft = m.sb("soft", [P, PAIRS, ROWS])
        keep = m.sb("keep", [P, ROWS])
        cum = m.sb("cum", [P, PAIRS, ROWS])
        ident = m.sb("ident", [P, P])
        t_ps = m.ps("t_ps", [P, 2, BLK])
        x_ps = m.ps("x_ps", [P, 4, BLK])
        loaded, consts, turned, copied = m.sem("loaded"), m.sem("consts"), m.sem("turned"), m.sem("copied")
        multiplied, biased = m.sem("multiplied"), m.sem("biased")
        s, v, keep_ready, stored = m.sem("scalar_step"), m.sem("vector_step"), m.sem("keep_ready"), m.sem("stored")
        block = stack.enter_context(nc.Block())

        @block.sync
        def _(sp):
            sp.dma_start(low[:], tail.rearrange("(t p) c -> p t c", p=P)[:, :, HEADS:TAIL]).then_inc(loaded, 16)
            sp.dma_start(up[:], w_up.rearrange("l r n -> (l r) n")).then_inc(loaded, 16)
            with nc.allow_non_contiguous_dma(reason="256 words"):
                sp.dma_start(bias[:], b_gla.rearrange("l (c p) -> p (l c)", p=P)).then_inc(loaded, 16)
            for c in range(PAIRS):
                sp.wait_ge(v, 3 * (c + 1))
                sp.dma_start(gla_cum[c], cum[:, c]).then_inc(stored, 16)
            sp.wait_ge(stored, 16 * PAIRS)

        @block.gpsimd
        def _(pool):
            make_identity(pool, ident, consts, consts)
            pool.memset(keep[:], 1.0).then_inc(keep_ready, 1)
            pool.wait_ge(keep_ready, 1)
            pool.memset(keep[:, 0:SEQ].rearrange("p (c t) -> p c t", t=P)[:, :, 0:1], 0.0).then_inc(keep_ready, 1)
            pool.memset(keep[:, SEQ:ROWS].rearrange("p (n t) -> p n t", t=DEC_SEQ)[:, :, 0:1], 0.0).then_inc(keep_ready, 1)

        @block.tensor
        def _(pe):
            pe.wait_ge(loaded, 48)
            pe.wait_ge(consts, 2)
            for n, (c0, w) in enumerate(COLS):
                if n >= 2:
                    pe.wait_ge(copied, n - 1)
                for t in range(w // P):
                    mm = pe.transpose(t_ps[0:LOW_RANK, n % 2, t * P:(t + 1) * P], low[:, c0 // P + t, :], ident[:])
                mm.then_inc(turned, 1)
            for n, (c0, w) in enumerate(COLS):
                pe.wait_ge(copied, n + 1)
                for c in range(PAIRS):
                    u = n * PAIRS + c
                    if u >= 4:
                        pe.wait_ge(biased, u - 3)
                    pe.matmul(x_ps[:, u % 4, 0:w], up[:, c * P:(c + 1) * P], lowT[:, c0:c0 + w], start=True, stop=True)\
                        .then_inc(multiplied, 1)

        @block.scalar
        def _(act):
            act.preload_act_table_set(TABLES)
            for n, (c0, w) in enumerate(COLS):
                for c in range(PAIRS):
                    act.wait_ge(multiplied, n * PAIRS + c + 1)
                    act.activation(x[:, c, c0:c0 + w], x_ps[:, (n * PAIRS + c) % 4, 0:w], ACT.Identity,
                                   bias=bias[:, c:c + 1]).then_inc(biased, 1)
            act.wait_ge(biased, PAIRS * len(COLS))
            for c in range(PAIRS):
                act.activation(mag[:, c], x[:, c], ACT.Abs).then_inc(s, 1)
                act.wait_ge(s, 3 * c + 1)
                act.activation(soft[:, c], mag[:, c], ACT.Exp, scale=-1.0).then_inc(s, 1)
                act.wait_ge(s, 3 * c + 2)
                act.activation(mag[:, c], soft[:, c], ACT.Ln, bias=1.0).then_inc(s, 1)

        @block.vector
        def _(dve):
            for n, (c0, w) in enumerate(COLS):
                dve.wait_ge(turned, n + 1)
                dve.tensor_copy(lowT[:, c0:c0 + w], t_ps[0:LOW_RANK, n % 2, 0:w]).then_inc(copied, 1)
            dve.wait_ge(keep_ready, 3)
            for c in range(PAIRS):
                dve.wait_ge(s, 3 * (c + 1))
                dve.tensor_scalar(x[:, c], x[:, c], 0.0, None, ALU.min).then_inc(v, 1)
                dve.wait_ge(v, 3 * c + 1)
                dve.tensor_tensor(x[:, c], x[:, c], mag[:, c], ALU.subtract).then_inc(v, 1)
                dve.wait_ge(v, 3 * c + 2)
                dve.tensor_tensor_scan(cum[:, c], keep[:], x[:, c], 0.0, ALU.mult, ALU.add).then_inc(v, 1)


def linear_attention(nc, z, gla_cum, state_gla, o_gla, gla_prompt, gla_sample):
    PAIRS = B_HEADS // 2
    CH = P
    HALVES = [CH >> (i + 1) for i in range(7)]
    S_HALVES = [h for h in HALVES if 2 * h <= DEC_SEQ]
    RING = 3
    PS_RING = 3
    INV_TAU = 1.0 / GLA_TAU
    with ExitStack() as stack:
        m = Pool(nc, stack, "gl")
        qk = m.sb("qk", [P, 2, 2 * D_BK])
        v_in = m.sb("v_in", [P, 2, D_B])
        b = m.sb("b", [P, 2, PAIRS, CH])
        q_bd = m.sb("q_bd", [P, 2, PAIRS, 2, CH])
        kT = m.sb("kT", [P, 2, PAIRS, CH])
        dist = m.sb("dist", [P, 2, PAIRS, CH])
        mag = m.sb("mag", [P, 2, PAIRS, CH])
        dec = m.sb("dec", [P, 2, PAIRS, CH])
        qE = m.sb("qE", [P, RING, PAIRS, 2, CH])
        kE = m.sb("kE", [P, RING, PAIRS, CH])
        q_in = m.sb("q_in", [P, PAIRS, 2, CH])
        exp_b = m.sb("exp_b", [P, PAIRS, CH])
        k_out = m.sb("k_out", [P, PAIRS, CH])
        k_tok = m.sb("k_tok", [P, PAIRS, P])
        att = m.sb("att", [P, B_HEADS, CH])
        o_sb = m.sb("o_sb", [P, D_B])
        state = m.sb("state", [P, PAIRS, B_VAL])
        s_state = m.sb("s_state", [P, DEC_BATCH, PAIRS, B_VAL])
        q_seq = m.sb("q_seq", [P, DEC_BATCH, B_HEADS, CH])
        k_seq = m.sb("k_seq", [P, DEC_BATCH, PAIRS, P])
        ones_i = m.sb("ones_i", [P, CH])
        masks = m.sb("masks", [P, len(HALVES) + 1, CH])
        own = m.sb("own", [P, DEC_BATCH])
        ident = m.sb("ident", [P, P])
        t_ps = m.ps("t_ps", [P, BLK])
        k_ps = m.ps("k_ps", [P, BLK])
        a_ps = m.ps("a_ps", [P, PS_RING, BLK])
        o_ps = m.ps("o_ps", [P, BLK])
        s_ps = m.ps("s_ps", [P, 2, BLK])

        consts, zeroed, filled = m.sem("consts"), m.sem("zeroed"), m.sem("filled")
        qkv_loaded = m.sems("qkv_loaded", 2)
        state_loaded = m.sem("state_loaded")
        turned = m.sem("turned")
        q_ready, k_ready = m.sem("q_ready"), m.sem("k_ready")
        apart = m.sem("apart")
        abs_done, dec_ready = m.sem("abs_done"), m.sem("dec_ready")
        qE_ready, kE_ready = m.sem("qE_ready"), m.sem("kE_ready")
        paired = m.sem("paired")
        kept = m.sem("kept")
        expb_ready, qin_ready = m.sem("expb_ready"), m.sem("qin_ready")
        kout_ready, k_turned, ktok_ready = m.sem("kout_ready"), m.sem("k_turned"), m.sem("ktok_ready")
        o_done, o_ready, o_stored = m.sem("o_done"), m.sem("o_ready"), m.sem("o_stored")
        grown, state_ready = m.sem("grown"), m.sem("state_ready")
        seq_ready = m.sem("seq_ready")
        out_stored = m.sem("out_stored")
        block = stack.enter_context(nc.Block())
        L = len(HALVES)
        U = L + 1
        D = L + 1
        LAST = PROMPT_TILES
        N_CONST = 2 * L + 3

        def blocks(x, n):
            return x.rearrange("p c (k n) -> p (c k) n", n=n)

        def chunks(step):
            def run(eng):
                with eng.Fori(0, PROMPT_TILES // 2) as i:
                    step(i * 2, 0, HALVES, CH)
                    step(i * 2 + 1, 1, HALVES, CH)
                step(LAST, 0, S_HALVES, DEC_SEQ)
            return run

        def half(hh):
            return slice(hh * B_KEY, (hh + 1) * B_KEY)

        @block.sync
        def _(sp):
            def load(c, par):
                rows = bass.ds(c * CH, CH)
                sp.dma_start(qk[:, par], z[Z_QKB, rows, :]).then_inc(qkv_loaded[par], 16)
                sp.dma_start(v_in[:, par], z[Z_VB, rows, :]).then_inc(qkv_loaded[par], 16)
                sp.dma_start(b[:, par], gla_cum[:, :, rows].rearrange("c p t -> p c t")).then_inc(qkv_loaded[par], 16)

            def store(c):
                sp.wait_ge(o_ready, c + 1)
                sp.dma_start(o_gla[bass.ds(c * CH, CH), :], o_sb[:]).then_inc(o_stored, 16)

            load(0, 0)
            load(1, 1)
            view = state_gla.rearrange("l n (c h) k e -> (l n) c (h k) e", h=2)
            for n in range(DEC_BATCH):
                sp.dma_start(s_state[:, n], view[n].rearrange("c p e -> p c e")).then_inc(state_loaded, 16)
            with sp.Fori(0, PROMPT_TILES // 2 - 1) as i:
                for par in range(2):
                    c = i * 2 + par
                    store(c)
                    sp.wait_ge(state_ready, c + 1)
                    load(c + 2, par)
            store(LAST - 2)
            sp.wait_ge(state_ready, LAST - 1)
            load(LAST, 0)
            store(LAST - 1)
            sp.wait_ge(state_ready, LAST)
            view = gla_prompt.rearrange("l b (c h) k e -> (l b c) (h k) e", h=2)
            sp.dma_start(view.rearrange("c p e -> p c e"), state[:]).then_inc(out_stored, 16)
            store(LAST)
            view = gla_sample.rearrange("l n (c h) k e -> (l n) c (h k) e", h=2)
            for n in range(DEC_BATCH):
                sp.wait_ge(state_ready, LAST + n + 1)
                sp.dma_start(view[n].rearrange("c p e -> p c e"), s_state[:, n]).then_inc(out_stored, 16)
            sp.wait_ge(o_stored, 16 * TILES)
            sp.wait_ge(out_stored, 16 * (DEC_BATCH + 1))

        @block.gpsimd
        def _(pool):
            make_identity(pool, ident, zeroed, zeroed)
            pool.memset(ones_i[:], 1.0).then_inc(zeroed, 1)
            pool.wait_ge(zeroed, 3)
            for i, h in enumerate(HALVES):
                k = CH // (2 * h)
                mk = masks[:, i].rearrange("p (k a) -> p k a", a=2 * h)[:, :, h:2 * h]
                pool.memset(masks[:, i], 0.0).then_inc(zeroed, 1)
                pool.wait_ge(zeroed, 4 + i)
                pool.affine_select(out=mk, in_=ones_i[:].rearrange("p (k a) -> p k a", a=2 * h)[:, :, h:2 * h],
                                   compare_op=ALU.is_ge, fill=0.0, base=0, pattern=[[-2 * h, k], [0, h]],
                                   channel_multiplier=1).then_inc(consts, 1)
                pool.wait_ge(consts, 2 * i + 1)
                pool.affine_select(out=mk, in_=mk, compare_op=ALU.is_ge, fill=0.0, base=h - 1,
                                   pattern=[[2 * h, k], [0, h]], channel_multiplier=-1).then_inc(consts, 1)
            pool.tensor_copy(masks[:, L], ident[:]).then_inc(consts, 1)
            pool.affine_select(out=own[:], in_=ones_i[:, 0:DEC_BATCH], compare_op=ALU.is_ge, fill=0.0, base=0,
                               pattern=[[-DEC_SEQ, DEC_BATCH]], channel_multiplier=1).then_inc(consts, 1)
            pool.wait_ge(consts, 2 * L + 2)
            pool.affine_select(out=own[:], in_=own[:], compare_op=ALU.is_ge, fill=0.0, base=DEC_SEQ - 1,
                               pattern=[[DEC_SEQ, DEC_BATCH]], channel_multiplier=-1).then_inc(consts, 1)

            def step(c, par, halves, n):
                pool.wait_ge(qkv_loaded[par], (c - par) * 24 + 48)

                def distance(i):
                    if i >= 2:
                        pool.wait_ge(abs_done, c * L + (i - 1))
                    else:
                        pool.wait_ge(dec_ready, c * D)
                    size, at = (2 * halves[i], halves[i] - 1) if i < len(halves) else (n, n - 1)
                    bb = blocks(b[:, par], size)
                    ref = bb[:, :, at:at + 1].broadcast_to([P, PAIRS * CH // size, size])
                    pool.tensor_tensor(blocks(dist[:, i % 2], size), bb, ref, ALU.subtract).then_inc(apart, 1)

                distance(0)
                pool.wait_ge(k_ready, c + 1)
                for i in range(len(halves)):
                    distance(i + 1)
                    pool.wait_ge(dec_ready, c * D + (i + 1))
                    pool.wait_ge(paired, c * U + (i + 2 - RING if i >= RING else 0))
                    pool.tensor_tensor(kE[:, i % RING], kT[:, par], dec[:, i % 2], ALU.mult).then_inc(kE_ready, 1)

            chunks(step)(pool)

        @block.scalar
        def _(act):
            act.preload_act_table_set(TABLES)
            act.wait_ge(filled, 6)

            def take_q(c, par):
                act.wait_ge(turned, c + 1)
                for hh in range(2):
                    src = t_ps[half(hh), 0:PAIRS * CH].rearrange("p (c t) -> p c t", c=PAIRS)
                    act.mul(q_bd[half(hh), par, :, hh, :], src, B_KEY ** -0.5).then_inc(q_ready, 1)

            def step(c, par, halves, n):
                for i in range(len(halves)):
                    act.wait_ge(apart, c * D + (i + 1))
                    act.wait_ge(dec_ready, c * D + max(i - 1, 0))
                    act.activation(mag[:, i % 2], dist[:, i % 2], ACT.Abs).then_inc(abs_done, 1)
                    act.wait_ge(abs_done, c * L + (i + 1))
                    act.wait_ge(qE_ready, c * (2 * L) + 2 * max(i - 1, 0))
                    act.wait_ge(kE_ready, c * L + max(i - 1, 0))
                    if i < 2:
                        act.wait_ge(kout_ready, c)
                    act.activation(dec[:, i % 2], mag[:, i % 2], ACT.Exp, scale=-INV_TAU).then_inc(dec_ready, 1)
                act.wait_ge(qin_ready, c * 2)
                act.wait_ge(state_ready, c)
                act.activation(exp_b[:], b[:, par], ACT.Exp, scale=INV_TAU).then_inc(expb_ready, 1)
                i = len(halves)
                act.wait_ge(apart, c * D + (i + 1))
                act.wait_ge(qE_ready, c * (2 * L) + 2 * (i - 1))
                act.wait_ge(kE_ready, c * L + (i - 1))
                act.activation(dec[:, i % 2], dist[:, i % 2], ACT.Exp, scale=-INV_TAU).then_inc(dec_ready, 1)
                if not (isinstance(c, int) and c == LAST):
                    take_q(c + 1, 1 - par)
                act.wait_ge(k_turned, c + 1)
                act.copy(k_tok[:].rearrange("p c k -> p (c k)"), k_ps[:, 0:D_BK]).then_inc(ktok_ready, 1)
                act.wait_ge(o_done, c + 1)
                act.wait_ge(o_stored, c * 16)
                act.copy(o_sb[:], o_ps[:]).then_inc(o_ready, 1)

            take_q(0, 0)
            chunks(step)(act)

        @block.vector
        def _(dve):
            for x in (q_bd, q_in, state, att, qE):
                dve.memset(x[:], 0.0).then_inc(filled, 1)
            dve.memset(q_seq[:], 0.0).then_inc(filled, 1)
            dve.wait_ge(filled, 6)
            dve.wait_ge(consts, N_CONST)

            def take_k(c, par):
                dve.wait_ge(turned, c + 1)
                dve.wait_ge(q_ready, c * 2 + 2)
                dve.tensor_copy(kT[:, par], t_ps[:, PAIRS * CH:].rearrange("p (c t) -> p c t", c=PAIRS)).then_inc(k_ready, 1)

            def step(c, par, halves, n):
                sample = isinstance(c, int) and c == LAST

                def keep(u):
                    dve.wait_ge(consts, N_CONST)
                    dve.wait_ge(paired, c * U + (u + 1))
                    if u == 0:
                        dve.wait_ge(o_done, c)
                    dve.wait_ge(kept, c * U + u)
                    mk = masks[:, L if u == 0 else HALVES.index(halves[u - 1])].bitcast(I32)
                    dve.copy_predicated(att[:], mk.unsqueeze(1).broadcast_to([P, B_HEADS, CH]),
                                        a_ps[:, u % PS_RING].rearrange("p (c t) -> p c t", c=B_HEADS)).then_inc(kept, 1)

                if sample:
                    dve.wait_ge(o_done, c)
                    dve.memset(att[:], 0.0).then_inc(filled, 1)
                    dve.wait_ge(filled, 7)
                dve.wait_ge(q_ready, c * 2 + 2)
                for i in range(len(halves)):
                    dve.wait_ge(dec_ready, c * D + (i + 1))
                    dve.wait_ge(paired, c * U + (i + 2 - RING if i >= RING else 0))
                    for hh in range(2):
                        dve.tensor_tensor(qE[half(hh), i % RING, :, hh, :], q_bd[half(hh), par, :, hh, :],
                                          dec[half(hh), i % 2], ALU.mult).then_inc(qE_ready, 1)
                    keep(i)
                dve.wait_ge(expb_ready, c + 1)
                dve.wait_ge(o_done, c)
                for hh in range(2):
                    dve.tensor_tensor(q_in[half(hh), :, hh, :], q_bd[half(hh), par, :, hh, :], exp_b[half(hh)],
                                      ALU.mult).then_inc(qin_ready, 1)
                dve.wait_ge(dec_ready, c * D + (len(halves) + 1))
                dve.wait_ge(k_turned, c)
                dve.tensor_tensor(k_out[:], kT[:, par], dec[:, len(halves) % 2], ALU.mult).then_inc(kout_ready, 1)
                keep(len(halves))
                if not sample:
                    take_k(c + 1, 1 - par)
                    dve.wait_ge(grown, c + 1)
                    dve.wait_ge(state_ready, c)
                    update(state, exp_b[:, :, CH - 1], s_ps[:, par])
                    return
                dve.wait_ge(qin_ready, c * 2 + 2)
                for s in range(DEC_BATCH):
                    cols = slice(s * DEC_SEQ, (s + 1) * DEC_SEQ)
                    dve.tensor_copy(q_seq[:, s, :, cols], q_in[:].rearrange("p c h t -> p (c h) t")[:, :, cols])\
                        .then_inc(seq_ready, 1)
                dve.wait_ge(ktok_ready, c + 1)
                for s in range(DEC_BATCH):
                    dve.tensor_scalar(k_seq[:, s], k_tok[:], own[:, s:s + 1], None, ALU.mult).then_inc(seq_ready, 1)
                dve.wait_ge(o_done, c + 1)
                for s in range(DEC_BATCH):
                    dve.wait_ge(grown, c + s + 1)
                    update(s_state[:, s], exp_b[:, :, (s + 1) * DEC_SEQ - 1], s_ps[:, s % 2])

            def update(st, scale, new):
                for pair in range(PAIRS):
                    for hh in range(2):
                        at = (pair * 2 + hh) * B_VAL
                        x = dve.scalar_tensor_tensor(out=st[half(hh), pair], in0=st[half(hh), pair], scalar=scale[half(hh), pair:pair + 1],
                                                     in1=new[half(hh), at:at + B_VAL], op0=ALU.mult, op1=ALU.add)
                x.then_inc(state_ready, 1)

            take_k(0, 0)
            chunks(step)(dve)

        @block.tensor
        def _(pe):
            pe.wait_ge(consts, N_CONST)
            pe.wait_ge(filled, 6)

            def turn(c, par):
                pe.wait_ge(qkv_loaded[par], (c - par) * 24 + 48)
                pe.wait_ge(k_ready, c)
                for x in range(2 * PAIRS):
                    mm = pe.transpose(t_ps[:, x * P:(x + 1) * P], qk[:, par, x * P:(x + 1) * P], ident[:])
                mm.then_inc(turned, 1)

            def step(c, par, halves, n):
                sample = isinstance(c, int) and c == LAST
                for u in range(len(halves) + 1):
                    i = u - 1
                    if u == 0:
                        pe.wait_ge(q_ready, c * 2 + 2)
                        pe.wait_ge(k_ready, c + 1)
                    else:
                        pe.wait_ge(qE_ready, c * (2 * L) + 2 * (i + 1))
                        pe.wait_ge(kE_ready, c * L + (i + 1))
                    pe.wait_ge(kept, c * U + (u + 1 - PS_RING if u >= PS_RING else 0))
                    for pair in range(PAIRS):
                        k_op = kT[:, par, pair] if u == 0 else kE[:, i % RING, pair]
                        q_op = q_bd[:, par, pair] if u == 0 else qE[:, i % RING, pair]
                        mm = pe.matmul(a_ps[:, u % PS_RING, pair * 2 * CH:(pair + 1) * 2 * CH], k_op,
                                       q_op.rearrange("p h t -> p (h t)"), start=True, stop=True)
                    mm.then_inc(paired, 1)
                if not sample:
                    turn(c + 1, 1 - par)
                pe.wait_ge(kout_ready, c + 1)
                pe.wait_ge(ktok_ready, c)
                for pair in range(PAIRS):
                    mm = pe.transpose(k_ps[:, pair * P:(pair + 1) * P], k_out[:, pair], ident[:])
                mm.then_inc(k_turned, 1)
                pe.wait_ge(kept, c * U + (len(halves) + 1))
                pe.wait_ge(qin_ready, c * 2 + 2)
                pe.wait_ge(o_ready, c)
                pe.wait_ge(state_ready, c)
                if sample:
                    pe.wait_ge(seq_ready, DEC_BATCH)
                    pe.wait_ge(state_loaded, 16 * DEC_BATCH)
                for h in range(B_HEADS):
                    out = o_ps[:, h * B_VAL:(h + 1) * B_VAL]
                    pe.matmul(out, att[:, h], v_in[:, par, h * B_VAL:(h + 1) * B_VAL], start=True, stop=False)
                    if not sample:
                        mm = pe.matmul(out, q_in[:, h // 2, h % 2], state[:, h // 2], start=False, stop=True)
                    else:
                        for s in range(DEC_BATCH):
                            mm = pe.matmul(out, q_seq[:, s, h], s_state[:, s, h // 2], start=False, stop=(s == DEC_BATCH - 1))
                mm.then_inc(o_done, 1)
                pe.wait_ge(ktok_ready, c + 1)

                def grow(k_op, slot):
                    for pair in range(PAIRS):
                        cols = slice(pair * 2 * B_VAL, (pair + 1) * 2 * B_VAL)
                        mm = pe.matmul(s_ps[:, slot, cols], k_op[:, pair], v_in[:, par, cols], start=True, stop=True)
                    mm.then_inc(grown, 1)

                if not sample:
                    grow(k_tok, par)
                else:
                    pe.wait_ge(seq_ready, 2 * DEC_BATCH)
                    for s in range(DEC_BATCH):
                        if s >= 2:
                            pe.wait_ge(state_ready, c + s - 1)
                        grow(k_seq[:, s], s % 2)

            turn(0, 0)
            chunks(step)(pe)


def attend_prompt(nc, z, decay_key, y_a):
    T = PROMPT_TILES
    AUG = HEAD_DIM + 3
    QG = 4
    GROUPS = T // QG
    NEG = -1.0e30
    MAX_UNITS = [[(i, c) for i in range(QG * g, QG * (g + 1)) for c in range(g + 1)] for g in range(GROUPS)]
    MAX_OF = {u: n for n, u in enumerate(u for us in MAX_UNITS for u in us)}
    FIN = [(g, j) for g in range(GROUPS) for j in range(QG * (g + 1))]
    N_MAX, N_FIN = len(MAX_OF), len(FIN)
    FIN_END = [sum(QG * (x + 1) for x in range(g + 1)) for g in range(GROUPS)]
    LAG = 2
    P_RING = 4
    TURNS = 3 * GROUPS
    with ExitStack() as stack:
        m = Pool(nc, stack, "pa")
        raw = m.sb("raw", [P, 2, 3, T, P])
        q_aug = m.sb("q_aug", [P, 2, T, AUG])
        k_aug = m.sb("k_aug", [P, 2, T, AUG])
        v_aug = m.sb("v_aug", [P, 2, T, HEAD_DIM + 1])
        decay = m.sb("decay", [P, 2, T, HEADS])
        kT = m.sb("kT", [P, 2, SEQ])
        kT_r = m.sb("kT_r", [P, 2, SEQ], F32R)
        qT = m.sb("qT", [P, 2, SEQ])
        qT_r = m.sb("qT_r", [P, 2, SEQ], F32R)
        probs = m.sb("probs", [P, P_RING, BLK])
        part_max = m.sb("part_max", [P, T, GROUPS])
        rden = m.sb("rden", [P, 2, QG])
        out = m.sb("out", [P, T, P])
        ident = m.sb("ident", [P, P])
        ident_b = m.sb("ident_b", [P, P], BF16)
        zero_b = m.sb("zero_b", [P, P], BF16)
        after_b = m.sb("after_b", [P, P], BF16)
        before_b = m.sb("before_b", [P, P], BF16)
        max_ps = m.ps("max_ps", [P, 2, BLK])
        st_ps = m.ps("st_ps", [P, 2, BLK])
        o_ps = m.ps("o_ps", [P, 2, BLK])
        t_ps = m.ps("t_ps", [P, 2, BLK])

        consts, padded = m.sem("consts"), m.sem("padded")
        decay_loaded = m.sem("decay_loaded")
        loaded = m.sems("loaded", 2)
        prepared = m.sem("prepared")
        decay_set = m.sem("decay_set")
        turned = m.sem("turned")
        copied_a = m.sem("copied_a")
        copied_v = m.sem("copied_v")
        k_rounded = m.sem("k_rounded")
        scored = m.sem("scored")
        reduced = m.sem("reduced")
        max_ready = m.sem("max_ready")
        st_done = m.sem("st_done")
        exp_done = m.sem("exp_done")
        pv_done = m.sem("pv_done")
        norm = m.sem("norm")
        o_ready = m.sem("o_ready")
        stored = m.sem("stored")
        block = stack.enter_context(nc.Block())

        def width(g, j):
            first = max(0, j - QG * g)
            return first, (QG - first) * P

        def start(do, h, hh):
            do.decay(h, hh)
            for c in range(2 * GROUPS):
                do.turn(h, hh, c)
            for u in MAX_UNITS[0]:
                do.maximum(h, hh, u)
            do.negate(h, hh, 0)
            do.turn(h, hh, 2 * GROUPS)

        def head(do, h, hh, last=False):
            for n, (g, j) in enumerate(FIN):
                do.score(h, hh, n)
                steps = QG * (g + 1)
                if g < GROUPS - 1:
                    per = 3 if g == 0 else 2
                    units = MAX_UNITS[g + 1][per * j:per * (j + 1)]
                    for u in units:
                        do.maximum(h, hh, u)
                    if units and units[-1] == MAX_UNITS[g + 1][-1]:
                        do.negate(h, hh, g + 1)
                elif not last:
                    if j == 0:
                        do.decay(h + 1, 1 - hh)
                    if j < 2 * GROUPS:
                        do.turn(h + 1, 1 - hh, j)
                    elif j < 2 * GROUPS + QG:
                        do.maximum(h + 1, 1 - hh, MAX_UNITS[0][j - 2 * GROUPS])
                        if j == 2 * GROUPS + QG - 1:
                            do.negate(h + 1, 1 - hh, 0)
                if n >= LAG:
                    do.weigh(h, hh, n - LAG)
                if j == steps - 1 and (g < GROUPS - 1 or not last):
                    following = (h, hh, 2 * GROUPS + g + 1) if g < GROUPS - 1 else (h + 1, 1 - hh, 2 * GROUPS)
                    do.turn(*following)
            for n in range(N_FIN - LAG, N_FIN):
                do.weigh(h, hh, n)

        def all_heads(eng, do):
            start(do, 0, 0)
            with eng.Fori(0, HEADS // 2 - 1) as pair:
                do.pair_begins(pair)
                head(do, pair * 2, 0)
                head(do, pair * 2 + 1, 1)
            do.pair_begins(HEADS // 2 - 1)
            head(do, HEADS - 2, 0)
            head(do, HEADS - 1, 1, last=True)

        class Part:

            def pair_begins(self, pair):
                pass

            decay = turn = maximum = negate = score = weigh = lambda self, *where: None

        @block.sync
        def _(sp):
            sp.dma_start(decay[:], decay_key.rearrange("a p (t h) -> p a t h", h=HEADS)).then_inc(decay_loaded, 16)

            def load(pair, slot):
                for n, b in enumerate((Z_QA, Z_KA, Z_VA)):
                    src = z[b, 0:SEQ, bass.ds(pair * P, P)].rearrange("(t p) c -> p t c", p=P)
                    sp.dma_start(raw[:, slot, n], src).then_inc(loaded[slot], 16)

            def store(pair):
                sp.wait_ge(o_ready, pair * (2 * GROUPS) + 2 * GROUPS)
                dst = y_a[0:SEQ, bass.ds(pair * P, P)].rearrange("(t p) c -> p t c", p=P)
                sp.dma_start(dst, out[:]).then_inc(stored, 16)

            load(0, 0)
            load(1, 1)
            for pair in range(HEADS // 2):
                if pair + 2 < HEADS // 2:
                    sp.wait_ge(prepared, pair * 6 + 6)
                    load(pair + 2, pair % 2)
                store(pair)
            sp.wait_ge(stored, 16 * (HEADS // 2))

        @block.gpsimd
        def _(pool):
            make_identity(pool, ident, consts, consts)
            pool.memset(zero_b[:], 0.0).then_inc(consts, 1)
            pool.memset(ident_b[:], 0.0).then_inc(consts, 1)
            pool.wait_ge(consts, 4)
            pool.affine_select(out=ident_b[:], in_=ident_b[:], compare_op=ALU.not_equal, fill=1.0, base=0,
                               pattern=[[-1, P]], channel_multiplier=1).then_inc(consts, 1)
            pool.affine_select(out=after_b[:], in_=zero_b[:], compare_op=ALU.is_ge, fill=NEG, base=0,
                               pattern=[[-1, P]], channel_multiplier=1).then_inc(consts, 1)
            pool.affine_select(out=before_b[:], in_=zero_b[:], compare_op=ALU.is_ge, fill=NEG, base=0,
                               pattern=[[1, P]], channel_multiplier=-1).then_inc(consts, 1)
            pool.memset(q_aug[:, :, :, HEAD_DIM:HEAD_DIM + 2], 1.0).then_inc(consts, 1)
            pool.memset(q_aug[:, :, :, HEAD_DIM + 2:HEAD_DIM + 3], 0.0).then_inc(consts, 1)
            pool.memset(k_aug[:, :, :, HEAD_DIM + 2:HEAD_DIM + 3], 1.0).then_inc(consts, 1)
            pool.memset(v_aug[:, :, :, HEAD_DIM:HEAD_DIM + 1], 1.0).then_inc(consts, 1)

            def prepare(h, hh, pair, slot, first=False):
                pool.wait_ge(loaded[slot], (pair - slot) * 24 + 48)
                if not first:
                    pool.wait_ge(pv_done, (h - 1) * N_FIN)
                cols = slice(hh * HEAD_DIM, (hh + 1) * HEAD_DIM)
                pool.tensor_scalar(q_aug[:, hh, :, 0:HEAD_DIM], raw[:, slot, 0, :, cols], HEAD_DIM ** -0.5, None,
                                   ALU.mult).then_inc(prepared, 1)
                pool.tensor_copy(k_aug[:, hh, :, 0:HEAD_DIM], raw[:, slot, 1, :, cols]).then_inc(prepared, 1)
                pool.tensor_copy(v_aug[:, hh, :, 0:HEAD_DIM], raw[:, slot, 2, :, cols]).then_inc(prepared, 1)

            prepare(0, 0, 0, 0, first=True)
            prepare(1, 1, 0, 0, first=True)
            for h in range(2, HEADS):
                prepare(h, h % 2, h // 2, h // 2 % 2)

        @block.scalar
        def _(act):
            act.preload_act_table_set(TABLES)
            act.wait_ge(padded, 4)

            class ScalarPart(Part):
                def turn(self, h, hh, c):
                    if GROUPS <= c < 2 * GROUPS:
                        return
                    n = c if c < GROUPS else c - GROUPS
                    dst, g = (kT, c) if c < GROUPS else (qT, c - 2 * GROUPS)
                    act.wait_ge(turned, h * TURNS + (c + 1))
                    if c == 0 and (not isinstance(h, int) or h >= 2):
                        act.wait_ge(pv_done, (h - 1) * N_FIN)
                    act.copy(dst[0:AUG, hh, g * BLK:(g + 1) * BLK], t_ps[0:AUG, c % 2, :]).then_inc(copied_a, 1)

                def score(self, h, hh, n):
                    _, w = width(*FIN[n])
                    act.wait_ge(st_done, h * N_FIN + (n + 1))
                    act.wait_ge(pv_done, h * N_FIN + max(n + 1 - P_RING, 0))
                    act.activation(probs[:, n % P_RING, 0:w], st_ps[:, n % 2, 0:w], ACT.Exp).then_inc(exp_done, 1)

            all_heads(act, ScalarPart())

        @block.vector
        def _(dve):
            for x in (kT[HEAD_DIM:P], kT_r[HEAD_DIM:P].bitcast(F32), qT_r[HEAD_DIM:P].bitcast(F32), qT[HEAD_DIM:P]):
                dve.memset(x, 0.0).then_inc(padded, 1)
            dve.wait_ge(padded, 4)
            dve.wait_ge(decay_loaded, 16)
            dve.wait_ge(consts, 11)

            class VectorPart(Part):
                def decay(self, h, hh):
                    if not isinstance(h, int) or h >= 1:
                        dve.wait_ge(turned, h * TURNS - (TURNS - 2 * GROUPS))
                    dve.tensor_copy(k_aug[:, hh, :, HEAD_DIM:HEAD_DIM + 2],
                                    decay[:, :, :, bass.ds(h, 1)].rearrange("p a t h -> p t (a h)")).then_inc(decay_set, 1)

                def turn(self, h, hh, c):
                    if c < GROUPS:
                        at = slice(c * BLK, (c + 1) * BLK)
                        dve.wait_ge(copied_a, h * (2 * GROUPS) + (c + 1))
                        dve.tensor_copy(kT_r[0:AUG - 1, hh, at], kT[0:AUG - 1, hh, at]).then_inc(k_rounded, 1)
                    elif c < 2 * GROUPS:
                        at = slice((c - GROUPS) * BLK, (c - GROUPS + 1) * BLK)
                        dve.wait_ge(turned, h * TURNS + (c + 1))
                        dve.tensor_copy(qT_r[0:AUG - 1, hh, at], t_ps[0:AUG - 1, c % 2, :]).then_inc(copied_v, 1)

                def maximum(self, h, hh, u):
                    i, c = u
                    n = MAX_OF[u]
                    dve.wait_ge(scored, h * N_MAX + (n + 1))
                    dve.tensor_reduce(part_max[:, i, c:c + 1], max_ps[:, n % 2, 0:min(BLK, (i + 1) * P - c * BLK)],
                                      AX.X, ALU.max).then_inc(reduced, 1)

                def negate(self, h, hh, g):
                    tiles = slice(QG * g, QG * (g + 1))
                    dve.wait_ge(reduced, h * N_MAX + (MAX_OF[MAX_UNITS[g][-1]] + 1))
                    dve.tensor_reduce(q_aug[:, hh, tiles, HEAD_DIM + 2], part_max[:, tiles, 0:g + 1], AX.X, ALU.max,
                                      negate=True).then_inc(max_ready, 1)

                def weigh(self, h, hh, n):
                    g, j = FIN[n]
                    if n + 1 != FIN_END[g]:
                        return
                    dve.wait_ge(pv_done, h * N_FIN + (n + 1))
                    o = o_ps[:, g % 2, 0:QG * (HEAD_DIM + 1)].rearrange("p (t c) -> p t c", t=QG)
                    dve.reciprocal(rden[:, g % 2], o[:, :, HEAD_DIM]).then_inc(norm, 1)
                    dve.wait_ge(norm, h * GROUPS + (g + 1))
                    if g == 0 and hh == 0:
                        dve.wait_ge(stored, self.pair * 16)
                    dst = out[:, QG * g:QG * (g + 1), hh * HEAD_DIM:(hh + 1) * HEAD_DIM]
                    dve.tensor_tensor(dst, o[:, :, 0:HEAD_DIM],
                                      rden[:, g % 2].unsqueeze(2).broadcast_to([P, QG, HEAD_DIM]), ALU.mult).then_inc(o_ready, 1)

                def pair_begins(self, pair):
                    self.pair = pair

            all_heads(dve, VectorPart())

        @block.tensor
        def _(pe):
            pe.wait_ge(consts, 11)
            pe.wait_ge(padded, 4)

            class TensorPart(Part):
                def turn(self, h, hh, c):
                    if c < 2:
                        pe.wait_ge(copied_a, h * (2 * GROUPS))
                    elif c - 2 < GROUPS:
                        pe.wait_ge(copied_a, h * (2 * GROUPS) + (c - 1))
                    elif c - 2 < 2 * GROUPS:
                        pe.wait_ge(copied_v, h * GROUPS + (c - 2 - GROUPS + 1))
                    else:
                        pe.wait_ge(copied_a, h * (2 * GROUPS) + (c - 1 - GROUPS))
                    if c == 0:
                        pe.wait_ge(prepared, h * 3 + 3)
                        pe.wait_ge(decay_set, h + 1)
                    if c >= 2 * GROUPS:
                        pe.wait_ge(max_ready, h * GROUPS + (c - 2 * GROUPS + 1))
                    src = k_aug if c < GROUPS else q_aug
                    for t in range(QG):
                        mm = pe.transpose(t_ps[0:AUG, c % 2, t * P:(t + 1) * P], src[:, hh, QG * (c % GROUPS) + t, :], ident[:])
                    mm.then_inc(turned, 1)

                def maximum(self, h, hh, u):
                    i, c = u
                    n = MAX_OF[u]
                    if n == 0:
                        pe.wait_ge(k_rounded, h * GROUPS + GROUPS)
                        pe.wait_ge(copied_v, h * GROUPS + GROUPS)
                    pe.wait_ge(reduced, h * N_MAX + max(n - 1, 0))
                    end = (i + 1) * P
                    w = min(BLK, end - c * BLK)
                    diag = c * BLK + w == end
                    o = max_ps[:, n % 2, 0:w]
                    mm = pe.matmul(o, qT_r[:, hh, i * P:end], kT_r[:, hh, c * BLK:c * BLK + w], start=True, stop=not diag)
                    if diag:
                        mm = pe.matmul(o[:, w - P:w], ident_b[:], after_b[:], start=False, stop=True)
                    mm.then_inc(scored, 1)

                def score(self, h, hh, n):
                    g, j = FIN[n]
                    first, w = width(g, j)
                    if j == 0:
                        pe.wait_ge(copied_a, h * (2 * GROUPS) + (GROUPS + g + 1))
                    pe.wait_ge(exp_done, h * N_FIN + max(n - 1, 0))
                    diag = j >= QG * g
                    q0 = (QG * g + first) * P
                    mm = pe.matmul(st_ps[:, n % 2, 0:w], kT[:, hh, j * P:(j + 1) * P], qT[:, hh, q0:q0 + w],
                                   start=True, stop=not diag)
                    if diag:
                        mm = pe.matmul(st_ps[:, n % 2, 0:P], ident_b[:], before_b[:], start=False, stop=True)
                    mm.then_inc(st_done, 1)

                def weigh(self, h, hh, n):
                    g, j = FIN[n]
                    first, _ = width(g, j)
                    pe.wait_ge(exp_done, h * N_FIN + (n + 1))
                    if j == 0:
                        pe.wait_ge(o_ready, h * GROUPS + max(g - 1, 0))
                    for t in range(first, QG):
                        mm = pe.matmul(o_ps[:, g % 2, t * (HEAD_DIM + 1):(t + 1) * (HEAD_DIM + 1)],
                                       probs[:, n % P_RING, (t - first) * P:(t - first + 1) * P], v_aug[:, hh, j, :],
                                       start=(j == 0 and t == 0), stop=(j == QG * g + t), skip_group_check=True)
                    mm.then_inc(pv_done, 1)

            all_heads(pe, TensorPart())


def page_decay(nc, cache_logf, page_table, logf, decay_past, decay_new):
    GROUPS = DEC_BATCH * N_PAGES // P
    SEQS = P // N_PAGES
    with ExitStack() as stack:
        m = Pool(nc, stack, "pd")
        pages = m.sb("pages", [P, GROUPS], I32)
        lf = m.sb("lf", [P, GROUPS, PAGE, HEADS])
        cum = m.sb("cum", [P, GROUPS, HEADS, PAGE])
        whole = m.sb("whole", [P, GROUPS, HEADS])
        rest = m.sb("rest", [P, GROUPS, HEADS])
        hi = m.sb("hi", [P, GROUPS, HEADS, PAGE], F32R)
        lf_new = m.sb("lf_new", [P, HEADS])
        hi_new = m.sb("hi_new", [HEADS, SAMPLE], F32R)
        neg_new = m.sb("neg_new", [HEADS, SAMPLE])
        ones = m.sb("ones", [P, P])
        later = m.sb("later", [P, P])
        upto = m.sb("upto", [P, SAMPLE])
        r_ps = m.ps("r_ps", [P, BLK])
        n_ps = m.ps("n_ps", [P, BLK])
        loaded, new_loaded, gathered = m.sem("loaded"), m.sem("new_loaded"), m.sems("gathered", GROUPS)
        consts, v, summed, stored = m.sem("consts"), m.sem("vector_step"), m.sem("summed"), m.sem("stored")
        block = stack.enter_context(nc.Block())
        SCANS = HEADS * GROUPS
        PER = 4

        @block.sync
        def _(sp):
            with nc.allow_non_contiguous_dma(reason="512 words"):
                sp.dma_start(pages[:], page_table.rearrange("(g s) n -> (s n) g", s=SEQS)).then_inc(loaded, 16)
            sp.dma_start(lf_new[:], logf[SEQ:ROWS, :]).then_inc(new_loaded, 16)
            for g in range(GROUPS):
                sp.wait_ge(v, SCANS + GROUPS + PER * (g + 1))
                for part, src in enumerate((hi[:, g].bitcast(F32), cum[:, g])):
                    for s in range(SEQS):
                        chunks = decay_past[(g * SEQS + s) * CHUNKS:(g * SEQS + s + 1) * CHUNKS, part * HEADS:(part + 1) * HEADS, :]
                        for j in range(CHUNK_PAGES):
                            dst = chunks[:, :, j * PAGE:(j + 1) * PAGE]
                            sp.dma_start(dst, src[s * N_PAGES + j:(s + 1) * N_PAGES:CHUNK_PAGES]).then_inc(stored, 16)
            sp.wait_ge(v, SCANS + GROUPS + PER * GROUPS + 3)
            sp.dma_start(decay_new[0:HEADS, :], hi_new[:].bitcast(F32)).then_inc(stored, 16)
            sp.dma_start(decay_new[HEADS:2 * HEADS, :], neg_new[:]).then_inc(stored, 16)
            sp.wait_ge(stored, 16 * (2 * DEC_BATCH * CHUNK_PAGES + 2))

        @block.gpsimd
        def _(pool):
            pool.wait_ge(loaded, 16)
            rows = cache_logf.rearrange("l n k h -> (l n) (k h)")
            for g in range(GROUPS):
                pool.indirect_dma_start(lf[:, g].rearrange("p k h -> p (k h)"), None, rows,
                                        bass.IndirectOffsetOnAxis(ap=pages[:, g:g + 1], axis=0)).then_inc(gathered[g], 16)
            pool.memset(ones[:], 1.0).then_inc(consts, 1)
            pool.wait_ge(consts, 1)
            pool.affine_select(out=later[:], in_=ones[:], compare_op=ALU.is_gt, fill=0.0, base=0,
                               pattern=[[-1, P]], channel_multiplier=1).then_inc(consts, 1)
            pool.wait_ge(consts, 2)
            pool.affine_select(out=later[:].rearrange("p (s n) -> p s n", s=SEQS), in_=later[:].rearrange("p (s n) -> p s n", s=SEQS),
                               compare_op=ALU.is_ge, fill=0.0, base=N_PAGES - 1, pattern=[[N_PAGES, SEQS], [0, N_PAGES]],
                               channel_multiplier=-1).then_inc(consts, 1)
            pool.affine_select(out=upto[:], in_=ones[:, 0:SAMPLE], compare_op=ALU.is_ge, fill=0.0, base=0,
                               pattern=[[1, SAMPLE]], channel_multiplier=-1).then_inc(consts, 1)
            pool.wait_ge(consts, 4)
            u = upto[:].rearrange("p (n t) -> p n t", t=DEC_SEQ)
            pool.affine_select(out=u, in_=u, compare_op=ALU.is_ge, fill=0.0, base=0,
                               pattern=[[-DEC_SEQ, DEC_BATCH], [0, DEC_SEQ]], channel_multiplier=1).then_inc(consts, 1)

        @block.vector
        def _(dve):
            for g in range(GROUPS):
                dve.wait_ge(gathered[g], 16)
                for h in range(HEADS):
                    dve.tensor_tensor_scan(cum[:, g, h], lf[:, g, :, h], lf[:, g, :, h], 0.0, ALU.add, ALU.bypass).then_inc(v, 1)
            for g in range(GROUPS):
                dve.wait_ge(v, HEADS * (g + 1))
                dve.tensor_copy(whole[:, g], cum[:, g, :, PAGE - 1]).then_inc(v, 1)
            base = SCANS + GROUPS
            dve.wait_ge(summed, 1)
            for g in range(GROUPS):
                dve.tensor_tensor(rest[:, g], r_ps[:, g * HEADS:(g + 1) * HEADS], whole[:, g], ALU.add).then_inc(v, 1)
                dve.wait_ge(v, base + PER * g + 1)
                dve.tensor_tensor(lf[:, g].rearrange("p k h -> p (k h)").rearrange("p (h k) -> p h k", h=HEADS),
                                  rest[:, g].unsqueeze(2).broadcast_to([P, HEADS, PAGE]), cum[:, g], ALU.subtract).then_inc(v, 1)
                dve.tensor_tensor(hi[:, g], rest[:, g].unsqueeze(2).broadcast_to([P, HEADS, PAGE]), cum[:, g],
                                  ALU.subtract).then_inc(v, 1)
                dve.wait_ge(v, base + PER * g + 3)
                dve.tensor_tensor(cum[:, g], lf[:, g].rearrange("p k h -> p (k h)").rearrange("p (h k) -> p h k", h=HEADS),
                                  hi[:, g].bitcast(F32), ALU.subtract).then_inc(v, 1)
            base += PER * GROUPS
            dve.wait_ge(summed, 2)
            dve.tensor_scalar(neg_new[:], n_ps[0:HEADS, 0:SAMPLE], -1.0, None, ALU.mult).then_inc(v, 1)
            dve.wait_ge(v, base + 1)
            dve.tensor_copy(hi_new[:], neg_new[:]).then_inc(v, 1)
            dve.wait_ge(v, base + 2)
            dve.tensor_tensor(neg_new[:], neg_new[:], hi_new[:].bitcast(F32), ALU.subtract).then_inc(v, 1)

        @block.tensor
        def _(pe):
            pe.wait_ge(consts, 5)
            pe.wait_ge(v, SCANS + GROUPS)
            pe.matmul(r_ps[:, 0:GROUPS * HEADS], later[:], whole[:].rearrange("p g h -> p (g h)"), start=True, stop=True).then_inc(summed, 1)
            pe.wait_ge(new_loaded, 16)
            pe.matmul(n_ps[0:HEADS, 0:SAMPLE], lf_new[0:SAMPLE], upto[0:SAMPLE], start=True, stop=True).then_inc(summed, 1)


def attend_sample(nc, z, cache_k, cache_v, page_table, decay_past, decay_new, y_a):
    CP = CHUNK_PAGES
    CK = CP * PAGE
    PAIRS = HEADS // 2
    R = HEADS * DEC_SEQ
    KEYS = PAST_LEN + SAMPLE
    NEG = -1.0e30
    with ExitStack() as stack:
        m = Pool(nc, stack, "sa")
        table = m.sb("table", [1, DEC_BATCH * N_PAGES], I32)
        pairs = m.sb("pairs", [1, (DEC_BATCH - 1) * CHUNKS, 2, CP], I32)
        tok = m.sb("tok", [P, 3, D_A])
        qT = m.sb("qT", [P, PAIRS, SAMPLE])
        qT_hi = m.sb("qT_hi", [P, PAIRS, SAMPLE], F32R)
        qT_lo = m.sb("qT_lo", [P, PAIRS, SAMPLE], F32R)
        kn_hi = m.sb("kn_hi", [P, PAIRS, SAMPLE], F32R)
        kn_lo = m.sb("kn_lo", [P, PAIRS, SAMPLE], F32R)
        vn_hi = m.sb("vn_hi", [P, D_A], F32R)
        vn_lo = m.sb("vn_lo", [P, D_A], F32R)
        q_both = m.sb("q_both", [P, 2, PAIRS, P], F32R)
        q_high = m.sb("q_high", [P, 2, PAIRS, P], F32R)
        k_raw = m.sb("k_raw", [P, 2, CP, D_A])
        v_raw = m.sb("v_raw", [P, 2, CP, D_A])
        kT_hi = m.sb("kT_hi", [P, 2, PAIRS, CK], F32R)
        kT_lo = m.sb("kT_lo", [P, 2, PAIRS, CK], F32R)
        v_hi = m.sb("v_hi", [P, 2, CP, D_A], F32R)
        v_lo = m.sb("v_lo", [P, 2, CP, D_A], F32R)
        addend = m.sb("addend", [P, 2, CK], F32R)
        addend_n = m.sb("addend_n", [P, SAMPLE], F32R)
        d_raw = m.sb("d_raw", [2 * HEADS, 2, CK])
        dn_raw = m.sb("dn_raw", [2 * HEADS, SAMPLE])
        scores = m.sb("scores", [P, KEYS])
        part_max = m.sb("part_max", [P, CHUNKS + 1])
        neg_max = m.sb("neg_max", [P, 1])
        probs = m.sb("probs", [P, 2, CK])
        part_sum = m.sb("part_sum", [P, CHUNKS + 1])
        total = m.sb("total", [P, 1])
        recip = m.sb("recip", [P, 1])
        p_both = m.sb("p_both", [P, 2, CP, P], F32R)
        p_high = m.sb("p_high", [P, 2, CP, P], F32R)
        o_halves = m.sb("o_halves", [P, D_A])
        o_sb = m.sb("o_sb", [P, D_A])
        ident = m.sb("ident", [P, P])
        lift = m.sb("lift", [P, P])
        lift_r = m.sb("lift_r", [P, P], F32R)
        fold = m.sb("fold", [P, P])
        spread = m.sb("spread", [DEC_SEQ, P])
        mask_q = m.sb("mask_q", [DEC_SEQ, DEC_BATCH, SAMPLE])
        mask = m.sb("mask", [P, DEC_BATCH, SAMPLE])
        t_ps = m.ps("t_ps", [P, 2, BLK])
        p_ps = m.ps("p_ps", [P, 2, BLK])
        s_ps = m.ps("s_ps", [P, 2, BLK])
        o_ps = m.ps("o_ps", [P, 2, BLK])

        table_loaded, tok_loaded = m.sem("table_loaded"), m.sem("tok_loaded")
        k_loaded, v_loaded = m.sems("k_loaded", 2), m.sems("v_loaded", 2)
        d_loaded = m.sems("d_loaded", 2)
        dn_loaded = m.sem("dn_loaded")
        made = m.sem("made")
        zeroed = m.sem("zeroed")
        lift_ready = m.sem("lift_ready")
        pre_turned, pre_scalar, pre_vector = m.sem("pre_turned"), m.sem("pre_scalar"), m.sem("pre_vector")
        mask_done, mask_ready = m.sem("mask_done"), m.sem("mask_ready")
        q_placed = m.sem("q_placed")
        turned = m.sem("turned")
        khi_ready, klo_ready = m.sem("khi_ready"), m.sem("klo_ready")
        scored = m.sem("scored")
        d_placed, dn_placed = m.sem("d_placed"), m.sem("dn_placed")
        moved = m.sem("moved")
        added = m.sem("added")
        taken = m.sem("taken")
        new_scored, new_moved = m.sem("new_scored"), m.sem("new_moved")
        new_added, new_taken, new_max = m.sem("new_added"), m.sem("new_taken"), m.sem("new_max")
        negated = m.sem("negated")
        exp_done = m.sem("exp_done")
        p_turned = m.sem("p_turned")
        phi_ready, plo_ready = m.sem("phi_ready"), m.sem("plo_ready")
        vhi_ready, vlo_ready = m.sem("vhi_ready"), m.sem("vlo_ready")
        weighed = m.sem("weighed")
        halves_ready, folded, o_ready = m.sem("halves_ready"), m.sem("folded"), m.sem("o_ready")
        summed, divided = m.sem("summed"), m.sem("divided")
        stored = m.sem("stored")
        pe_waited, pool_waited = m.sem("pe_waited"), m.sem("pool_waited")
        block = stack.enter_context(nc.Block())
        W = CHUNKS + 1
        MADE = 15
        ZEROED = 6
        PLACED = 6 * PAIRS

        def rows(par):
            return slice(par * R, (par + 1) * R)

        class Part:
            begin_keys = step = end_keys = begin_values = end_values = finish = lambda self, *where: None

        def schedule(eng, do):
            def loop(n, par, keys, values):
                do.step(n, par, 0, 0, keys, values)
                do.step(n, par, 1, 1, keys, values)
                with eng.Fori(1, CHUNKS // 2 - 1) as i:
                    do.step(n, par, i * 2, 0, keys, values)
                    do.step(n, par, i * 2 + 1, 1, keys, values)
                do.step(n, par, CHUNKS - 2, 0, keys, values)
                do.step(n, par, CHUNKS - 1, 1, keys, values)

            def two(n, par):
                do.begin_keys(n, par)
                loop(n, par, True, True)
                do.end_keys(n, par)
                do.end_values(n - 1, 1 - par)
                do.begin_values(n, par)
                do.finish(n - 1, 1 - par)

            do.begin_keys(0, 0)
            loop(0, 0, True, False)
            do.end_keys(0, 0)
            do.begin_values(0, 0)
            with eng.Fori(0, DEC_BATCH // 2 - 1) as i:
                two(i * 2 + 1, 1)
                two(i * 2 + 2, 0)
            two(DEC_BATCH - 1, 1)
            loop(DEC_BATCH, 0, False, True)
            do.end_values(DEC_BATCH - 1, 1)
            do.finish(DEC_BATCH - 1, 1)

        def is_first(c):
            return isinstance(c, int) and c == 0

        def is_last(c):
            return isinstance(c, int) and c == CHUNKS - 1

        @block.sync
        def _(sp):
            sp.dma_start(table[:], page_table.rearrange("n p -> (n p)").unsqueeze(0)).then_inc(table_loaded, 16)
            for part, seqs in enumerate((slice(1, DEC_BATCH), slice(0, DEC_BATCH - 1))):
                src = page_table[seqs].rearrange("n (c j) -> (n c) j", j=CP)
                sp.dma_start(pairs[:, :, part], src.unsqueeze(0)).then_inc(table_loaded, 16)
            for i, b in enumerate((Z_QA, Z_KA, Z_VA)):
                sp.dma_start(tok[:, i], z[b, SEQ:ROWS, :]).then_inc(tok_loaded, 16)
            sp.dma_start(dn_raw[:], decay_new).then_inc(dn_loaded, 16)
            sp.wait_ge(table_loaded, 48)
            k_view = cache_k.rearrange("l n k h d -> (l n) k (h d)")
            v_view = cache_v.rearrange("l n k h d -> (l n) k (h d)")
            n_pool = k_view.shape[0]

            def numbers(x):
                _, pages = nc.values_load_multi_w_load_instructions(x, engines=(mybir.EngineType.SP,), min_val=0, max_val=n_pool - 1,
                                                                    skip_runtime_bounds_check_because="page_table holds numbers of pages of the pool")
                return pages

            def find(chunk):
                return numbers(table[0:1, bass.ds(chunk * CP, CP)])

            def find_both(chunk):
                both = numbers(pairs[0:1, bass.ds(chunk, 1)].rearrange("a c t j -> a (c t j)"))
                return both[:CP], both[CP:]

            def page(at, j, dst, view, sem):
                sp.dma_start(dst[:, j], view[bass.ds(at, 1)].rearrange("a k x -> (a k) x")).then_inc(sem, 16)

            def load_k(k, slot, pages, first=False):
                for j in range(CP):
                    if not first:
                        sp.wait_ge(turned, (k - 2) * CP + (j + 1))
                    page(pages[j], j, k_raw[:, slot], k_view, k_loaded[slot])

            def load_v(v, slot, pages, first=False):
                if not first:
                    sp.wait_ge(vhi_ready, v - 1)
                for j in range(CP):
                    if not first and j % (CP // 2) == 0:
                        sp.wait_ge(vlo_ready, (v - 2) * 2 + (1 if j == 0 else 2))
                    page(pages[j], j, v_raw[:, slot], v_view, v_loaded[slot])

            ALL = DEC_BATCH * CHUNKS
            for slot in range(2):
                load_k(slot, slot, find(slot), first=True)
            for slot in range(2):
                load_v(slot, slot, find(slot), first=True)
            with sp.Fori(1, CHUNKS // 2 + 1) as i:
                for slot in range(2):
                    load_k(i * 2 + slot, slot, find(i * 2 + slot))
            with sp.Fori(1, (ALL - CHUNKS) // 2) as i:
                for slot in range(2):
                    k_pages, v_pages = find_both(i * 2 + slot)
                    load_k(i * 2 + (slot + CHUNKS), slot, k_pages)
                    load_v(i * 2 + slot, slot, v_pages)
            with sp.Fori((ALL - CHUNKS) // 2, ALL // 2) as i:
                for slot in range(2):
                    load_v(i * 2 + slot, slot, find(i * 2 + slot))

        @block.gpsimd
        def _(pool):
            count = [0]

            def then(ins):
                ins.then_inc(made, 1)
                count[0] += 1
                pool.wait_ge(made, count[0])

            def one_where(x, base, pattern):
                then(pool.affine_select(out=x, in_=x, compare_op=ALU.not_equal, fill=1.0, base=base, pattern=pattern,
                                        channel_multiplier=1))

            for x in (ident, lift, fold, spread):
                then(pool.memset(x[:], 0.0))
            one_where(ident[:], 0, [[-1, P]])
            by_head = lift[:, 0:R].rearrange("p (h q) -> p h q", q=DEC_SEQ)
            one_where(by_head, 0, [[-1, HEADS], [0, DEC_SEQ]])
            one_where(by_head, -HEADS, [[-1, HEADS], [0, DEC_SEQ]])
            one_where(lift[:, 0:R], -R, [[-1, R]])
            for base in (-R, 0, R):
                one_where(fold[:], base, [[-1, P]])
            one_where(spread[:].rearrange("p (h q) -> p h q", q=DEC_SEQ), 0, [[0, P // DEC_SEQ], [-1, DEC_SEQ]])
            then(pool.memset(mask_q[:], 0.0))
            then(pool.affine_select(out=mask_q[:], in_=mask_q[:], compare_op=ALU.is_ge, fill=NEG, base=0,
                                    pattern=[[-DEC_SEQ, DEC_BATCH], [1, SAMPLE]], channel_multiplier=0))
            then(pool.affine_select(out=mask_q[:], in_=mask_q[:], compare_op=ALU.is_ge, fill=NEG, base=0,
                                    pattern=[[DEC_SEQ, DEC_BATCH], [-1, SAMPLE]], channel_multiplier=1))
            assert count[0] == MADE
            pool.wait_ge(zeroed, ZEROED)
            pool.wait_ge(pre_vector, 2)

            class PoolPart(Part):
                def begin_keys(self, n, par):
                    if not (isinstance(n, int) and n == 0):
                        pool.wait_ge(scored, (n - 1) * CHUNKS)
                        pool.wait_ge(vlo_ready, (n - 1) * (2 * CHUNKS))
                    toks = bass.ds(n * DEC_SEQ, DEC_SEQ)
                    for hh in range(2):
                        part = slice(hh * HEAD_DIM, (hh + 1) * HEAD_DIM)
                        for pair in range(PAIRS):
                            at = (pair * 2 + hh) * DEC_SEQ
                            for dst, c0, src in ((q_both, 0, qT_hi), (q_both, R, qT_lo), (q_high, 0, qT_hi)):
                                pool.tensor_copy(dst[part, par, pair, c0 + at:c0 + at + DEC_SEQ],
                                                 src[part, pair, toks].bitcast(F32)).then_inc(q_placed, 1)
                        pool.wait_ge(q_placed, n * PLACED + (hh + 1) * (PLACED // 2))
                        pool.sem_inc(pool_waited, 1)

                def step(self, n, par, c, slot, keys, values):
                    if not values:
                        return
                    pool.wait_ge(vhi_ready, (n - 1) * CHUNKS + c + 1)
                    pool.wait_ge(weighed, (n - 1) * W + c)
                    for part in (slice(0, CP // 2), slice(CP // 2, CP)):
                        pool.tensor_tensor(v_lo[:, slot, part], v_raw[:, slot, part], v_hi[:, slot, part].bitcast(F32),
                                           ALU.subtract).then_inc(vlo_ready, 1)

            schedule(pool, PoolPart())

        @block.scalar
        def _(act):
            act.preload_act_table_set(TABLES)
            t4 = lambda x: x.rearrange("p (c t) -> p c t", c=PAIRS)[:, :, 0:SAMPLE]
            act.wait_ge(pre_turned, 1)
            act.mul(qT[:], t4(t_ps[:, 0]), HEAD_DIM ** -0.5).then_inc(pre_scalar, 1)
            act.wait_ge(pre_turned, 2)
            act.copy(kn_hi[:], t4(t_ps[:, 1])).then_inc(pre_scalar, 1)
            act.wait_ge(mask_done, 1)
            act.copy(mask[:].rearrange("p n t -> p (n t)"), o_ps[:, 0]).then_inc(mask_ready, 1)
            act.wait_ge(zeroed, ZEROED)
            act.wait_ge(dn_loaded, 16)
            act.copy(addend_n[0:2 * HEADS], dn_raw[:]).then_inc(dn_placed, 1)

            def load_d(k, slot):
                if isinstance(k, int) and k >= DEC_BATCH * CHUNKS:
                    return
                src = decay_past[bass.ds(k, 1)].rearrange("a h k -> (a h) k")
                act.dma_start(d_raw[:, slot], src).then_inc(d_loaded[slot], 16)

            load_d(0, 0)
            load_d(1, 1)

            class ScalarPart(Part):
                def high(self, n, c, slot, j):
                    act.wait_ge(turned, n * (CHUNKS * CP) + c * CP + (j + 1))
                    act.copy(kT_hi[:, slot, :, j * PAGE:(j + 1) * PAGE],
                             t_ps[:, j % 2].rearrange("p (c k) -> p c k", c=PAIRS)).then_inc(khi_ready, 1)

                def place(self, n, c, slot):
                    act.wait_ge(d_loaded[slot], n * (16 * CHUNKS // 2) + (c - slot) * 8 + 16)
                    act.wait_ge(added, n * CHUNKS + c)
                    act.copy(addend[0:2 * HEADS, slot], d_raw[:, slot]).then_inc(d_placed, 1)

                def fetch(self, n, c, slot):
                    act.wait_ge(d_placed, n * CHUNKS + c + 1)
                    load_d(n * CHUNKS + (c + 2), slot)

                def move(self, n, c, slot):
                    act.wait_ge(scored, n * CHUNKS + c + 1)
                    act.copy(addend[R:P, slot], s_ps[R:P, slot]).then_inc(moved, 1)

                def step(self, n, par, c, slot, keys, values):
                    e = (n - 1) * W + c
                    if keys:
                        self.high(n, c, slot, 0)
                        if not is_first(c):
                            self.place(n, c - 1, 1 - slot)
                    if values and is_last(c):
                        self.exp_new(n - 1, 1 - par)
                    elif values:
                        self.exp_chunk(n - 1, 1 - par, c + 1, 1 - slot, (n - 1) * W + c)
                    if keys:
                        self.high(n, c, slot, 1)
                    if values:
                        self.halves(e, slot, P, CP)
                    if keys:
                        if not is_first(c):
                            self.move(n, c - 1, 1 - slot)
                        if is_last(c):
                            act.wait_ge(new_scored, n + 1)
                            act.copy(addend_n[R:P], s_ps[R:P, 1, 0:SAMPLE]).then_inc(new_moved, 1)
                        self.high(n, c, slot, 2)
                        self.high(n, c, slot, 3)
                        if not is_first(c):
                            self.fetch(n, c - 1, 1 - slot)

                def end_keys(self, n, par):
                    self.place(n, CHUNKS - 1, 1)
                    self.fetch(n, CHUNKS - 1, 1)
                    self.move(n, CHUNKS - 1, 1)

                def exp(self, n, par, free, slot, src, w, column):
                    act.wait_ge(negated, n + 1)
                    act.wait_ge(p_turned, free)
                    act.activation(probs[rows(par), slot, 0:w], src, ACT.Exp, bias=neg_max[rows(par), 0:1],
                                   accum_out=column).then_inc(exp_done, 1)

                def halves(self, e, slot, keys, count):
                    act.wait_ge(p_turned, e + 1)
                    src = p_ps[0:keys, slot, 0:count * R].rearrange("p (j r) -> p j r", j=count)
                    act.copy(p_both[0:keys, slot, 0:count, 0:R], src).then_inc(phi_ready, 1)
                    act.copy(p_high[0:keys, slot, 0:count, 0:R], src).then_inc(phi_ready, 1)

                def exp_chunk(self, n, par, c, slot, free):
                    self.exp(n, par, free, slot, scores[rows(par), bass.ds(c * CK, CK)], CK, part_sum[rows(par), bass.ds(c, 1)])

                def exp_new(self, n, par):
                    self.exp(n, par, n * W + (CHUNKS - 1), 0, scores[rows(par), PAST_LEN:KEYS], SAMPLE, part_sum[rows(par), CHUNKS:W])

                def begin_values(self, n, par):
                    self.exp_chunk(n, par, 0, 0, n * W)

                def end_values(self, n, par):
                    self.halves(n * W + CHUNKS, 0, SAMPLE, 1)

                def finish(self, n, par):
                    act.wait_ge(o_ready, n + 1)
                    for h in range(HEADS):
                        dst = y_a[bass.ds(n * DEC_SEQ + SEQ, DEC_SEQ), h * HEAD_DIM:(h + 1) * HEAD_DIM]
                        act.dma_start(dst, o_sb[par * R + h * DEC_SEQ:par * R + (h + 1) * DEC_SEQ,
                                                h * HEAD_DIM:(h + 1) * HEAD_DIM]).then_inc(stored, 16)

            schedule(act, ScalarPart())
            act.wait_ge(stored, 16 * HEADS * DEC_BATCH)

        @block.vector
        def _(dve):
            dve.memset(scores[:, 0:2 * PAIRS * P], 0.0).then_inc(zeroed, 1)
            dve.wait_ge(zeroed, 1)
            for x in (q_both[:].rearrange("p a b c -> p (a b c)"), q_high[:].rearrange("p a b c -> p (a b c)"),
                      addend[:].rearrange("p a b -> p (a b)"), addend_n[:], p_high[:].rearrange("p a b c -> p (a b c)")):
                dve.tensor_copy(x, scores[:, 0:x.shape[1]]).then_inc(zeroed, 1)
            dve.wait_ge(made, MADE)
            dve.tensor_copy(lift_r[:], lift[:]).then_inc(lift_ready, 1)
            dve.wait_ge(pre_scalar, 1)
            dve.tensor_copy(qT_hi[:], qT[:]).then_inc(pre_vector, 1)
            dve.wait_ge(pre_vector, 1)
            dve.tensor_tensor(qT_lo[:], qT[:], qT_hi[:].bitcast(F32), ALU.subtract).then_inc(pre_vector, 1)
            dve.wait_ge(pre_scalar, 2)
            dve.tensor_tensor(kn_lo[:], t_ps[:, 1].rearrange("p (c t) -> p c t", c=PAIRS)[:, :, 0:SAMPLE],
                              kn_hi[:].bitcast(F32), ALU.subtract).then_inc(pre_vector, 1)
            dve.wait_ge(tok_loaded, 48)
            dve.tensor_copy(vn_hi[:], tok[:, 2]).then_inc(pre_vector, 1)
            dve.wait_ge(pre_vector, 4)
            dve.tensor_tensor(vn_lo[:], tok[:, 2], vn_hi[:].bitcast(F32), ALU.subtract).then_inc(pre_vector, 1)
            dve.wait_ge(mask_ready, 1)
            dve.wait_ge(zeroed, ZEROED)

            class VectorPart(Part):
                def low_keys(self, n, c, slot, j):
                    dve.wait_ge(khi_ready, n * (CHUNKS * CP) + c * CP + (j + 1))
                    at = slice(j * PAGE, (j + 1) * PAGE)
                    dve.tensor_tensor(kT_lo[:, slot, :, at], t_ps[:, j % 2].rearrange("p (c k) -> p c k", c=PAIRS),
                                      kT_hi[:, slot, :, at].bitcast(F32), ALU.subtract).then_inc(klo_ready, 1)

                def take(self, n, par, c, slot):
                    dve.wait_ge(added, n * CHUNKS + c + 1)
                    dve.tensor_scalar(scores[rows(par), bass.ds(c * CK, CK)], s_ps[0:R, slot], 1.0, None, ALU.mult, ALU.max,
                                      accum_out=part_max[rows(par), bass.ds(c, 1)]).then_inc(taken, 1)

                def high_values(self, v, e, slot, c):
                    dve.wait_ge(v_loaded[slot], v * (16 * CP * CHUNKS // 2) + (c - slot) * (8 * CP) + 16 * CP)
                    dve.wait_ge(weighed, e)
                    dve.tensor_copy(v_hi[:, slot], v_raw[:, slot]).then_inc(vhi_ready, 1)

                def step(self, n, par, c, slot, keys, values):
                    e = (n - 1) * W + c
                    if keys:
                        self.low_keys(n, c, slot, 0)
                    if values:
                        self.high_values(n - 1, e, slot, c)
                    if keys:
                        self.low_keys(n, c, slot, 1)
                    if values:
                        self.low(e, slot, P, CP)
                    if keys:
                        self.low_keys(n, c, slot, 2)
                        self.low_keys(n, c, slot, 3)
                        if not is_first(c):
                            self.take(n, par, c - 1, 1 - slot)
                        if is_last(c):
                            self.take_new(n, par)

                def end_keys(self, n, par):
                    self.take(n, par, CHUNKS - 1, 1)
                    dve.wait_ge(new_max, n + 1)
                    dve.wait_ge(taken, (n + 1) * CHUNKS)
                    dve.tensor_reduce(neg_max[rows(par)], part_max[rows(par)], AX.X, ALU.max, negate=True).then_inc(negated, 1)

                def take_new(self, n, par):
                    dve.wait_ge(new_added, n + 1)
                    dve.tensor_tensor(scores[rows(par), PAST_LEN:KEYS], s_ps[0:R, 1, 0:SAMPLE],
                                      mask[0:R, bass.ds(n, 1)].rearrange("p a t -> p (a t)"), ALU.add).then_inc(new_taken, 1)
                    dve.wait_ge(new_taken, n + 1)
                    dve.tensor_reduce(part_max[rows(par), CHUNKS:W], scores[rows(par), PAST_LEN:KEYS], AX.X, ALU.max).then_inc(new_max, 1)

                def low(self, e, slot, keys, count):
                    dve.wait_ge(phi_ready, e * 2 + 2)
                    dve.tensor_tensor(p_both[0:keys, slot, 0:count, R:P],
                                      p_ps[0:keys, slot, 0:count * R].rearrange("p (j r) -> p j r", j=count),
                                      p_both[0:keys, slot, 0:count, 0:R].bitcast(F32), ALU.subtract).then_inc(plo_ready, 1)

                def end_values(self, n, par):
                    self.low(n * W + CHUNKS, 0, SAMPLE, 1)
                    dve.wait_ge(weighed, n * W + (W + 1))
                    dve.tensor_copy(o_halves[:], o_ps[:, par]).then_inc(halves_ready, 1)
                    dve.wait_ge(exp_done, n * W + W)
                    dve.tensor_reduce(total[rows(par)], part_sum[rows(par)], AX.X, ALU.add).then_inc(summed, 1)
                    dve.wait_ge(summed, n + 1)
                    dve.reciprocal(recip[rows(par)], total[rows(par)]).then_inc(divided, 1)
                    dve.wait_ge(divided, n + 1)
                    dve.wait_ge(folded, n + 1)
                    if not (isinstance(n, int) and n == 0):
                        dve.wait_ge(stored, (n - par) * (16 * HEADS))
                    dve.tensor_scalar(o_sb[rows(par)], p_ps[rows(par), 0], recip[rows(par), 0:1], None, ALU.mult).then_inc(o_ready, 1)

            schedule(dve, VectorPart())

        @block.tensor
        def _(pe):
            pe.wait_ge(made, MADE)
            pe.wait_ge(tok_loaded, 48)
            for i in range(2):
                for pair in range(PAIRS):
                    mm = pe.transpose(t_ps[:, i, pair * P:(pair + 1) * P], tok[:, i, pair * P:(pair + 1) * P], ident[:])
                mm.then_inc(pre_turned, 1)
            pe.matmul(o_ps[:, 0], spread[:], mask_q[:].rearrange("p n t -> p (n t)"), start=True, stop=True).then_inc(mask_done, 1)
            pe.wait_ge(pre_scalar, 2)
            pe.wait_ge(pre_vector, 5)
            pe.wait_ge(zeroed, ZEROED)
            pe.wait_ge(lift_ready, 1)
            pe.wait_ge(mask_ready, 1)
            pe.sem_inc(weighed, 1)

            class TensorPart(Part):
                def turn(self, n, c, slot, j):
                    if j == 0:
                        pe.wait_ge(k_loaded[slot], n * (16 * CP * CHUNKS // 2) + (c - slot) * (8 * CP) + 16 * CP)
                    wait_from(pe, klo_ready, n * (CHUNKS * CP) + c * CP + (j - 1))
                    for pair in range(PAIRS):
                        mm = pe.transpose(t_ps[:, j % 2, pair * PAGE:(pair + 1) * PAGE],
                                          k_raw[:, slot, j, pair * P:(pair + 1) * P], ident[:])
                    mm.then_inc(turned, 1)

                def score(self, par, out, hi, lo):
                    for pair in range(PAIRS):
                        pe.matmul(out, q_both[:, par, pair], hi(pair), start=(pair == 0), stop=False, skip_group_check=True)
                        mm = pe.matmul(out, q_high[:, par, pair], lo(pair), start=False, stop=(pair == PAIRS - 1), skip_group_check=True)
                    return mm

                def first_passes(self, n, par, c, slot):
                    pe.wait_ge(klo_ready, n * (CHUNKS * CP) + c * CP + CP)
                    pe.wait_ge(q_placed, n * PLACED + PLACED)
                    pe.wait_ge(taken, n * CHUNKS + c)
                    pe.wait_ge(new_taken, n)
                    self.score(par, s_ps[:, slot], lambda pair: kT_hi[:, slot, pair], lambda pair: kT_lo[:, slot, pair]).then_inc(scored, 1)

                def third_pass(self, n, c, slot):
                    pe.wait_ge(moved, n * CHUNKS + c + 1)
                    pe.wait_ge(d_placed, n * CHUNKS + c + 1)
                    pe.matmul(s_ps[:, slot], lift_r[:], addend[:, slot], start=False, stop=True, skip_group_check=True).then_inc(added, 1)

                def step(self, n, par, c, slot, keys, values):
                    e = (n - 1) * W + c
                    score, weigh = keys and not is_first(c), values and not is_first(c)
                    if keys:
                        self.turn(n, c, slot, 0)
                        self.turn(n, c, slot, 1)
                    if values:
                        if is_first(c) and not (isinstance(n, int) and n == 1):
                            pe.wait_ge(o_ready, n - 1)
                        self.turn_weights(1 - par, e, slot, CP, P, e if is_first(c) else e - 1)
                    if score:
                        self.first_passes(n, par, c - 1, 1 - slot)
                    if keys and is_last(c):
                        self.score_new(n, par)
                    if keys:
                        self.turn(n, c, slot, 2)
                    if weigh:
                        self.weigh(1 - par, n - 1, c - 1, 1 - slot, range(0, CP // 2))
                    if keys:
                        self.turn(n, c, slot, 3)
                    if score:
                        self.third_pass(n, c - 1, 1 - slot)
                    if keys and is_last(c):
                        pe.wait_ge(new_moved, n + 1)
                        pe.wait_ge(dn_placed, 1)
                        pe.matmul(s_ps[:, 1, 0:SAMPLE], lift_r[:], addend_n[:], start=False, stop=True, skip_group_check=True).then_inc(new_added, 1)
                    if weigh:
                        self.weigh(1 - par, n - 1, c - 1, 1 - slot, range(CP // 2, CP))

                def score_new(self, n, par):
                    pe.wait_ge(taken, n * CHUNKS + (CHUNKS - 2))
                    self.score(par, s_ps[:, 1, 0:SAMPLE], lambda pair: kn_hi[:, pair], lambda pair: kn_lo[:, pair]).then_inc(new_scored, 1)

                def end_keys(self, n, par):
                    pe.wait_ge(new_taken, n + 1)
                    self.first_passes(n, par, CHUNKS - 1, 1)
                    self.third_pass(n, CHUNKS - 1, 1)

                def turn_weights(self, par, e, slot, count, keys, free):
                    pe.wait_ge(exp_done, e + 1)
                    wait_from(pe, plo_ready, free)
                    pe.sem_inc(pe_waited, 1)
                    for j in range(count):
                        mm = pe.transpose(p_ps[0:keys, slot, j * R:(j + 1) * R], probs[rows(par), slot, j * keys:(j + 1) * keys],
                                          ident[rows(par), rows(par)])
                    mm.then_inc(p_turned, 1)

                def weigh(self, par, n, c, slot, pages):
                    if 0 in pages:
                        pe.wait_ge(plo_ready, n * W + c + 1)
                        pe.wait_ge(vlo_ready, n * (2 * CHUNKS) + c * 2 + 2)
                    for j in pages:
                        end = j == CP - 1
                        pe.matmul(o_ps[:, par], p_both[:, slot, j], v_hi[:, slot, j], start=(is_first(c) and j == 0), stop=False, skip_group_check=True)
                        mm = pe.matmul(o_ps[:, par], p_high[:, slot, j], v_lo[:, slot, j], start=False, stop=end, skip_group_check=True)
                    if end:
                        mm.then_inc(weighed, 1)

                def end_values(self, n, par):
                    e = n * W + CHUNKS
                    self.turn_weights(par, e, 0, 1, SAMPLE, e - 1)
                    self.weigh(par, n, CHUNKS - 1, 1, range(CP))
                    pe.wait_ge(plo_ready, e + 1)
                    k = slice(0, SAMPLE)
                    pe.matmul(o_ps[:, par], p_both[k, 0, 0], vn_hi[k], start=False, stop=False, skip_group_check=True)
                    pe.matmul(o_ps[:, par], p_high[k, 0, 0], vn_lo[k], start=False, stop=True, skip_group_check=True).then_inc(weighed, 1)
                    pe.wait_ge(halves_ready, n + 1)
                    pe.wait_ge(plo_ready, n * W + W)
                    pe.matmul(p_ps[:, 0], fold[:], o_halves[:], start=True, stop=True).then_inc(folded, 1)

            schedule(pe, TensorPart())


def conv_inputs(nc, z, state_conv, ext_prompt, ext_sample, conv_prompt, conv_sample, k_prompt, v_prompt, k_sample, v_sample):
    HALO = CONV_W - 1
    PER = SEQ // P
    PART = PER // 4
    with ExitStack() as stack:
        m = Pool(nc, stack, "ci")
        cc = m.sb("cc", [P, PER, D_C])
        xc = m.sb("xc", [P, PER, D_C])
        sample = m.sb("sample", [SAMPLE, 2, D_C])
        zeros = m.sb("zeros", [HALO, D_C])
        loaded = m.sems("loaded", 4)
        sample_loaded = m.sem("sample_loaded")
        zeroed = m.sem("zeroed")
        product = m.sem("product")
        ext_stored, state_stored = m.sem("ext_stored"), m.sem("state_stored")
        copied = m.sem("copied")
        block = stack.enter_context(nc.Block())
        own = slice(SEQ, SEQ + SAMPLE)

        @block.sync
        def _(sp):
            sp.dma_start(ext_sample[:, 0:HALO], state_conv.rearrange("l n w c -> (l n) w c")).then_inc(state_stored, 16)
            for i in range(4):
                part = slice(i * PART, (i + 1) * PART)
                for dst, b in ((cc, Z_CC), (xc, Z_XC)):
                    src = z[b, 0:SEQ, :].rearrange("(p t) n -> p t n", p=P)
                    sp.dma_start(dst[:, part], src[:, part]).then_inc(loaded[i], 16)
            for i, b in enumerate((Z_CC, Z_XC)):
                sp.dma_start(sample[:, i], z[b, own, :]).then_inc(sample_loaded, 16)
            flat = lambda x: x.rearrange("l n t h d -> (l n t) (h d)")
            for dst, b, rows in ((k_prompt, Z_KA, slice(0, SEQ)), (v_prompt, Z_VA, slice(0, SEQ)),
                                 (k_sample, Z_KA, own), (v_sample, Z_VA, own)):
                sp.dma_start(flat(dst), z[b, rows, :]).then_inc(copied, 16)
            sp.wait_ge(zeroed, 1)
            sp.dma_start(ext_prompt[0:HALO], zeros[:]).then_inc(ext_stored, 16)
            body = ext_prompt[HALO:HALO + SEQ].rearrange("(p t) n -> p t n", p=P)
            for i in range(4):
                part = slice(i * PART, (i + 1) * PART)
                sp.wait_ge(product, i + 1)
                sp.dma_start(body[:, part], xc[:, part]).then_inc(ext_stored, 16)
            sp.wait_ge(product, 5)
            sp.dma_start(ext_sample[:, HALO:HALO + DEC_SEQ], sample[:, 1]).then_inc(ext_stored, 16)
            sp.wait_ge(ext_stored, 16 * 6)
            sp.wait_ge(state_stored, 16)
            sp.dma_start(conv_prompt.rearrange("l n w c -> (l n w) c"), ext_prompt[SEQ:SEQ + HALO]).then_inc(copied, 16)
            sp.dma_start(conv_sample.rearrange("l n w c -> (l n) w c"), ext_sample[:, DEC_SEQ:DEC_SEQ + HALO]).then_inc(copied, 16)
            sp.wait_ge(copied, 16 * 6)

        @block.vector
        def _(dve):
            dve.memset(zeros[:], 0.0).then_inc(zeroed, 1)
            for i in range(4):
                part = slice(i * PART, (i + 1) * PART)
                dve.wait_ge(loaded[i], 32)
                dve.tensor_tensor(xc[:, part], cc[:, part], xc[:, part], ALU.mult).then_inc(product, 1)
            dve.wait_ge(sample_loaded, 32)
            dve.tensor_tensor(sample[:, 1], sample[:, 0], sample[:, 1], ALU.mult).then_inc(product, 1)


def wait_from(eng, sem, count):
    if not isinstance(count, int) or count > 0:
        eng.wait_ge(sem, count)


def each_tile(eng, step):
    step(0, 0)
    step(1, 1)
    with eng.Fori(1, PROMPT_TILES // 2) as i:
        step(i * 2, 0)
        step(i * 2 + 1, 1)
    step(TILES - 1, 0)


def is_last(t):
    return isinstance(t, int) and t == TILES - 1


def merge_branches(nc, z, y_a, o_gla, ext_prompt, ext_sample, g_gla, conv_w, branches, merged_out):
    CH = D_A // P
    UNITS = 3
    IN = 9
    EXT = 6
    NH = D_MODEL // BLK
    with ExitStack() as stack:
        m = Pool(nc, stack, "mb")
        ident = m.sb("ident", [P, P])
        eps = m.sb("eps", [P, 1])
        w_hi = m.sb("w_hi", [P, UNITS, CH, D_MODEL], F32R)
        w_lo = m.sb("w_lo", [P, UNITS, CH, D_MODEL], F32R)
        taps = m.sb("taps", [P, CONV_W, D_C])
        gain = m.sb("gain", [P, D_B])
        inp = m.sb("inp", [P, 2, IN, BLK])
        mg = m.sb("mg", [P, 2, UNITS, D_MODEL])
        e = m.sb("e", [P, UNITS, BLK])
        square = m.sb("square", [P, B_HEADS, B_VAL])
        sumsq = m.sb("sumsq", [P, 2, B_HEADS])
        log_ms = m.sb("log_ms", [P, 2, B_HEADS])
        rstd = m.sb("rstd", [P, 2, B_HEADS])
        conv = m.sb("conv", [P, D_C])
        tap = m.sb("tap", [P, D_C])
        h_hi = m.sb("h_hi", [P, 2, CH, P], F32R)
        h_lo = m.sb("h_lo", [P, 2, CH, P], F32R)
        gated = m.sb("gated", [P, UNITS, D_MODEL])
        merged = m.sb("merged", [P, 2, D_MODEL])
        t_ps = m.ps("t_ps", [P, 2, CH, P])
        acc = m.ps("acc", [P, UNITS, NH, BLK])

        zeroed, ident_ready, const_ready = m.sem("zeroed"), m.sem("ident_ready"), m.sem("const_ready")
        w_loaded, whi_ready, wlo_ready = m.sems("w_loaded", 2), m.sem("whi_ready"), m.sem("wlo_ready")
        loaded, mg_loaded = m.sems("loaded", 2), m.sems("mg_loaded", 2 * UNITS)
        e_ready = m.sem("e_ready")
        squared, logged, rstd_ready = m.sem("squared"), m.sem("logged"), m.sem("rstd_ready")
        mg_ready = m.sem("mg_ready")
        sig = m.sem("sig")
        tapped = m.sem("tapped")
        stepped = m.sem("stepped")
        y_ready, turned = m.sem("y_ready"), m.sem("turned")
        hi_ready, lo_ready = m.sem("hi_ready"), m.sem("lo_ready")
        acc_done, gated_done = m.sem("acc_done"), m.sem("gated_done")
        added, merged_ready = m.sem("added"), m.sem("merged_ready")
        stored = m.sems("stored", 2)
        block = stack.enter_context(nc.Block())
        raw = [inp[:, 1].rearrange("p i n -> p (i n)")[:, h * CH // 2 * D_MODEL:(h + 1) * CH // 2 * D_MODEL]
               .rearrange("p (k n) -> p k n", n=D_MODEL) for h in range(2)]
        CONV_STEPS = 2 * CONV_W - 1
        Y_STEPS = 3

        @block.sync
        def _(sp):
            def load(t, par):
                rows = bass.ds(t * P, P)
                n = SAMPLE if is_last(t) else P
                one = lambda b: z[b, rows, :]
                wait_from(sp, turned, t * UNITS - UNITS)
                sp.dma_start(inp[0:n, par, 0], y_a[bass.ds(t * P, n), :]).then_inc(loaded[par], 16)
                sp.dma_start(inp[:, par, 1], o_gla[rows, :]).then_inc(loaded[par], 16)
                for i, b in ((2, Z_BC), (3, Z_GA), (4, Z_GB), (5, Z_GC)):
                    sp.dma_start(inp[:, par, i], one(b)).then_inc(loaded[par], 16)
                for i in range(CONV_W):
                    src = ext_sample[:, i:i + DEC_SEQ] if is_last(t) else ext_prompt[bass.ds(t * P + i, P), :]
                    sp.dma_start(inp[0:n, par, EXT + i], src).then_inc(loaded[par], 16)

            def load_mg(t, par, i):
                wait_from(sp, gated_done, t * UNITS + (i + 1 - 2 * UNITS))
                src = z[Z_MG + NH * i:Z_MG + NH * (i + 1), bass.ds(t * P, P), :].rearrange("b p n -> p b n")
                sp.dma_start(mg[:, par, i].rearrange("p (h n) -> p h n", n=BLK), src).then_inc(mg_loaded[UNITS * par + i], 16)

            sp.dma_start(gain[:], g_gla.rearrange("l n -> (l n)").partition_broadcast(P)).then_inc(const_ready, 16)
            sp.dma_start(taps[:], conv_w.rearrange("l w c -> (l w) c").partition_broadcast(P)).then_inc(const_ready, 16)
            load(0, 0)
            for par in range(2):
                for i in range(UNITS):
                    load_mg(par, par, i)
            for i, w in enumerate(branches):
                src = w.rearrange("l (k p) n -> p (l k) n", p=P)
                for h in range(2):
                    if i > 0:
                        sp.wait_ge(whi_ready, 2 * i + h - 1)
                        sp.wait_ge(wlo_ready, 2 * i + h - 1)
                    sp.dma_start(raw[h], src[:, h * CH // 2:(h + 1) * CH // 2]).then_inc(w_loaded[h], 16)
            sp.wait_ge(whi_ready, 2 * UNITS)
            sp.wait_ge(wlo_ready, 2 * UNITS)
            load(1, 1)

            def store(t, par):
                sp.wait_ge(merged_ready, t + 1)
                n = SAMPLE if is_last(t) else P
                sp.dma_start(merged_out[bass.ds(t * P, n), :], merged[0:n, par]).then_inc(stored[par], 16)

            def step(t, par):
                load(t + 2, par)
                for i in range(UNITS):
                    load_mg(t + 2, par, i)
                store(t, par)

            with sp.Fori(0, PROMPT_TILES // 2 - 1) as i:
                step(i * 2, 0)
                step(i * 2 + 1, 1)
            step(TILES - 3, 0)
            store(TILES - 2, 1)
            store(TILES - 1, 0)
            sp.wait_ge(stored[0], 16 * (PROMPT_TILES // 2 + 1))
            sp.wait_ge(stored[1], 16 * (PROMPT_TILES // 2))

        @block.gpsimd
        def _(pool):
            make_identity(pool, ident, zeroed, ident_ready)
            pool.memset(eps[:], EPS).then_inc(const_ready, 16)
            pool.wait_ge(const_ready, 48)

            def convolve(t, par):
                pool.wait_ge(loaded[par], (t - par) * (8 * IN) + 16 * IN)
                wait_from(pool, y_ready, t * UNITS)
                at = t * CONV_STEPS
                pool.tensor_tensor(conv[:], inp[:, par, EXT], taps[:, 0], ALU.mult).then_inc(tapped, 1)
                for i in range(1, CONV_W):
                    pool.tensor_tensor(tap[:], inp[:, par, EXT + i], taps[:, i], ALU.mult).then_inc(tapped, 1)
                    pool.wait_ge(tapped, at + 2 * i)
                    pool.tensor_tensor(conv[:], conv[:], tap[:], ALU.add).then_inc(tapped, 1)
                    pool.wait_ge(tapped, at + (2 * i + 1))

            def add(t, par):
                pool.wait_ge(gated_done, t * UNITS + 2)
                wait_from(pool, stored[par], (t - par) * 8)
                pool.tensor_tensor(merged[:, par], gated[:, 0], gated[:, 1], ALU.add).then_inc(added, 1)
                pool.wait_ge(gated_done, t * UNITS + 3)
                pool.wait_ge(added, t + 1)
                pool.tensor_tensor(merged[:, par], merged[:, par], gated[:, 2], ALU.add).then_inc(merged_ready, 1)

            convolve(0, 0)

            def step(t, par):
                if not is_last(t):
                    convolve(t + 1, 1 - par)
                add(t, par)

            each_tile(pool, step)

        @block.scalar
        def _(act):
            act.preload_act_table_set(TABLES)
            act.wait_ge(const_ready, 48)

            SIGMOIDS = 2 * (1 + UNITS)

            def sigmoid(before, out, x, ready):
                act.activation(out, x, ACT.Exp, scale=-1.0).then_inc(sig, 1)
                act.wait_ge(sig, before + 1)
                act.activation(out, out, ACT.Ln, bias=1.0).then_inc(sig, 1)
                act.wait_ge(sig, before + 2)
                act.activation(out, out, ACT.Exp, scale=-1.0).then_inc(ready, 1)

            def gate_exps(t, par):
                act.wait_ge(loaded[par], (t - par) * (8 * IN) + 16 * IN)
                for h in range(B_HEADS):
                    act.activation(square[:, h], inp[:, par, 1, h * B_VAL:(h + 1) * B_VAL], ACT.Square,
                                   accum_out=sumsq[:, par, h:h + 1]).then_inc(squared, 1)
                wait_from(act, y_ready, t * UNITS + (1 - UNITS))
                sigmoid(t * SIGMOIDS, e[:], inp[:, par, 3:6], e_ready)
                act.wait_ge(squared, t * B_HEADS + B_HEADS)
                act.activation(log_ms[:, par], sumsq[:, par], ACT.Ln, bias=eps[:, 0:1], scale=1.0 / B_VAL).then_inc(logged, 1)
                act.wait_ge(logged, t + 1)
                act.activation(rstd[:, par], log_ms[:, par], ACT.Exp, scale=-0.5).then_inc(rstd_ready, 1)

            def gate_sigmoid(t, par, i):
                act.wait_ge(mg_loaded[UNITS * par + i], (t - par) * 8 + 16)
                sigmoid(t * SIGMOIDS + (2 + 2 * i), mg[:, par, i], mg[:, par, i], mg_ready)

            def high(u, slot):
                act.wait_ge(turned, u + 1)
                wait_from(act, acc_done, u - 1)
                act.copy(h_hi[:, slot], t_ps[:, slot]).then_inc(hi_ready, 1)

            gate_exps(0, 0)
            for i in range(UNITS):
                for h in range(2):
                    act.wait_ge(w_loaded[h], 16 * (i + 1))
                    act.copy(w_hi[:, i, h * CH // 2:(h + 1) * CH // 2], raw[h]).then_inc(whi_ready, 1)
            for i in range(UNITS):
                gate_sigmoid(0, 0, i)
            high(0, 0)

            def step(t, par):
                high(t * UNITS + 1, 1 - par)
                if not is_last(t):
                    gate_exps(t + 1, 1 - par)
                high(t * UNITS + 2, par)
                if not is_last(t):
                    gate_sigmoid(t + 1, 1 - par, 0)
                    high(t * UNITS + 3, 1 - par)
                    gate_sigmoid(t + 1, 1 - par, 1)
                    gate_sigmoid(t + 1, 1 - par, 2)

            each_tile(act, step)

        @block.vector
        def _(dve):
            dve.wait_ge(const_ready, 48)

            def make_y(t, par, i):
                at = t * Y_STEPS
                gates = inp[:, par, 3:6]
                if i == 0:
                    dve.wait_ge(e_ready, t + 1)
                    dve.tensor_tensor(gates, gates, e[:], ALU.mult).then_inc(stepped, 1)
                    dve.wait_ge(stepped, at + 1)
                    dve.tensor_tensor(inp[:, par, 0], inp[:, par, 0], inp[:, par, 3], ALU.mult).then_inc(y_ready, 1)
                elif i == 1:
                    dve.wait_ge(rstd_ready, t + 1)
                    for h in range(B_HEADS):
                        c = slice(h * B_VAL, (h + 1) * B_VAL)
                        last = dve.scalar_tensor_tensor(out=inp[:, par, 1, c], in0=inp[:, par, 1, c], scalar=rstd[:, par, h:h + 1],
                                                        in1=gain[:, c], op0=ALU.mult, op1=ALU.mult)
                    last.then_inc(stepped, 1)
                    dve.wait_ge(stepped, at + 2)
                    dve.tensor_tensor(inp[:, par, 1], inp[:, par, 1], inp[:, par, 4], ALU.mult).then_inc(y_ready, 1)
                else:
                    dve.tensor_tensor(inp[:, par, 2], inp[:, par, 2], inp[:, par, 5], ALU.mult).then_inc(stepped, 1)
                    dve.wait_ge(stepped, at + 3)
                    dve.wait_ge(tapped, t * CONV_STEPS + CONV_STEPS)
                    dve.tensor_tensor(inp[:, par, 2], inp[:, par, 2], conv[:], ALU.mult).then_inc(y_ready, 1)

            def low(u, slot):
                dve.wait_ge(hi_ready, u + 1)
                dve.tensor_tensor(h_lo[:, slot], t_ps[:, slot], h_hi[:, slot].bitcast(F32), ALU.subtract).then_inc(lo_ready, 1)

            def gate(t, par, i):
                u = t * UNITS + i
                dve.wait_ge(acc_done, u + 1)
                dve.wait_ge(mg_ready, u + 1)
                wait_from(dve, merged_ready, t)
                dve.tensor_tensor(gated[:, i], acc[:, i].rearrange("p h n -> p (h n)"), mg[:, par, i], ALU.mult).then_inc(gated_done, 1)

            make_y(0, 0, 0)
            make_y(0, 0, 1)
            for i in range(UNITS):
                for h in range(2):
                    part = slice(h * CH // 2, (h + 1) * CH // 2)
                    dve.wait_ge(whi_ready, 2 * i + h + 1)
                    dve.tensor_tensor(w_lo[:, i, part], raw[h], w_hi[:, i, part].bitcast(F32), ALU.subtract).then_inc(wlo_ready, 1)
            low(0, 0)

            def step(t, par):
                last = is_last(t)
                for i in range(UNITS):
                    if not (last and i == 2):
                        low(t * UNITS + (i + 1), (par + i + 1) % 2)
                    if i == 0:
                        make_y(t, par, 2)
                    elif not last:
                        make_y(t + 1, 1 - par, i - 1)
                    gate(t, par, i)

            each_tile(dve, step)

        @block.tensor
        def _(pe):
            pe.wait_ge(ident_ready, 1)

            def turn(u, slot, par, i):
                pe.wait_ge(y_ready, u + 1)
                wait_from(pe, lo_ready, u - 1)
                for k in range(CH):
                    mm = pe.transpose(t_ps[:, slot, k], inp[:, par, i, k * P:(k + 1) * P], ident[:])
                mm.then_inc(turned, 1)

            turn(0, 0, 0, 0)
            pe.wait_ge(wlo_ready, 2 * UNITS)

            def step(t, par):
                for i in range(UNITS):
                    u = t * UNITS + i
                    slot = (par + i) % 2
                    if not (is_last(t) and i == 2):
                        turn(t * UNITS + (i + 1), 1 - slot, par if i < 2 else 1 - par, (i + 1) % UNITS)
                    pe.wait_ge(lo_ready, u + 1)
                    wait_from(pe, gated_done, u - 2)
                    for h in range(NH):
                        terms = [(a, b, k) for k in range(CH) for a, b in ((h_hi, w_hi), (h_hi, w_lo), (h_lo, w_hi))]
                        for q, (a, b, k) in enumerate(terms):
                            mm = pe.matmul(acc[:, i, h], a[:, slot, k], b[:, i, k, h * BLK:(h + 1) * BLK],
                                           start=(q == 0), stop=(q == len(terms) - 1))
                    mm.then_inc(acc_done, 1)

            each_tile(pe, step)


def project_out(nc, x_all, merged, w_out, g_final, y_prompt, y_sample):
    NH = D_MODEL // BLK
    with ExitStack() as stack:
        m = Pool(nc, stack, "po")
        ident = m.sb("ident", [P, P])
        eps = m.sb("eps", [P, 1])
        gain = m.sb("gain", [P, D_MODEL])
        w_hi = m.sb("w_hi", [P, KC, D_MODEL], F32R)
        w_lo = m.sb("w_lo", [P, KC, D_MODEL], F32R)
        w_raw = m.sb("w_raw", [P, KC, D_MODEL])
        m_in = m.sb("m_in", [P, 2, D_MODEL])
        x_in = m.sb("x_in", [P, 2, D_MODEL])
        h_hi = m.sb("h_hi", [P, 2, KC, P], F32R)
        h_lo = m.sb("h_lo", [P, 2, KC, P], F32R)
        out = m.sb("out", [P, 2, D_MODEL])
        square = m.sb("square", [P, D_MODEL])
        y = m.sb("y", [P, 2, D_MODEL])
        sumsq, log_ms, rstd = m.sb("sumsq", [P, 2]), m.sb("log_ms", [P, 2]), m.sb("rstd", [P, 2])
        t_ps = m.ps("t_ps", [P, 2, KC, P])
        acc = m.ps("acc", [P, 2, D_MODEL])

        zeroed, ident_ready, const_ready = m.sem("zeroed"), m.sem("ident_ready"), m.sem("const_ready")
        w_loaded, whi_ready, wlo_ready = m.sem("w_loaded"), m.sem("whi_ready"), m.sem("wlo_ready")
        m_loaded, x_loaded = m.sems("m_loaded", 2), m.sems("x_loaded", 2)
        turned, hi_ready, lo_ready = m.sem("turned"), m.sem("hi_ready"), m.sem("lo_ready")
        acc_done, out_ready = m.sem("acc_done"), m.sem("out_ready")
        squared, logged, rstd_ready = m.sem("squared"), m.sem("logged"), m.sem("rstd_ready")
        y_ready = m.sem("y_ready")
        stored = m.sems("stored", 2)
        block = stack.enter_context(nc.Block())

        @block.sync
        def _(sp):
            sp.dma_start(gain[:], g_final.partition_broadcast(P)).then_inc(const_ready, 16)

            def load(t, par):
                n = SAMPLE if is_last(t) else P
                wait_from(sp, turned, t - 1)
                sp.dma_start(m_in[0:n, par], merged[bass.ds(t * P, n), :]).then_inc(m_loaded[par], 16)
                wait_from(sp, out_ready, t - 1)
                sp.dma_start(x_in[:, par], x_all[bass.ds(t * P, P), :]).then_inc(x_loaded[par], 16)

            def store(t, par):
                sp.wait_ge(y_ready, t + 1)
                if is_last(t):
                    sp.dma_start(y_sample.rearrange("n t d -> (n t) d"), y[0:SAMPLE, par]).then_inc(stored[par], 16)
                else:
                    dst = y_prompt.rearrange("n t d -> (n t) d")[bass.ds(t * P, P), :]
                    sp.dma_start(dst, y[:, par]).then_inc(stored[par], 16)

            load(0, 0)
            for k in range(KC):
                sp.dma_start(w_raw[:, k], w_out[0, k * P:(k + 1) * P, :]).then_inc(w_loaded, 16)
            load(1, 1)

            def step(t, par):
                load(t + 2, par)
                store(t, par)

            with sp.Fori(0, PROMPT_TILES // 2 - 1) as i:
                step(i * 2, 0)
                step(i * 2 + 1, 1)
            step(TILES - 3, 0)
            store(TILES - 2, 1)
            store(TILES - 1, 0)
            sp.wait_ge(stored[0], 16 * (PROMPT_TILES // 2 + 1))
            sp.wait_ge(stored[1], 16 * (PROMPT_TILES // 2))

        @block.gpsimd
        def _(pool):
            make_identity(pool, ident, zeroed, ident_ready)
            pool.memset(eps[:], EPS).then_inc(const_ready, 16)

        @block.scalar
        def _(act):
            act.preload_act_table_set(TABLES)
            act.wait_ge(const_ready, 32)

            def high(t, par):
                act.wait_ge(turned, t + 1)
                wait_from(act, acc_done, t - 1)
                act.copy(h_hi[:, par], t_ps[:, par]).then_inc(hi_ready, 1)

            high(0, 0)
            act.wait_ge(w_loaded, 16 * KC)
            for k in range(2):
                part = slice(k * KC // 2, (k + 1) * KC // 2)
                act.copy(w_hi[:, part], w_raw[:, part]).then_inc(whi_ready, 1)

            def step(t, par):
                if not is_last(t):
                    high(t + 1, 1 - par)
                act.wait_ge(out_ready, t + 1)
                act.activation(square[:], out[:, par], ACT.Square, accum_out=sumsq[:, par:par + 1]).then_inc(squared, 1)
                act.wait_ge(squared, t + 1)
                act.activation(log_ms[:, par:par + 1], sumsq[:, par:par + 1], ACT.Ln, bias=eps[:, 0:1], scale=1.0 / D_MODEL).then_inc(logged, 1)
                act.wait_ge(logged, t + 1)
                wait_from(act, y_ready, t - 1)
                act.activation(rstd[:, par:par + 1], log_ms[:, par:par + 1], ACT.Exp, scale=-0.5).then_inc(rstd_ready, 1)

            each_tile(act, step)

        @block.vector
        def _(dve):
            dve.wait_ge(const_ready, 32)

            def low(t, par):
                dve.wait_ge(hi_ready, t + 1)
                dve.tensor_tensor(h_lo[:, par], t_ps[:, par], h_hi[:, par].bitcast(F32), ALU.subtract).then_inc(lo_ready, 1)

            low(0, 0)
            for k in range(2):
                part = slice(k * KC // 2, (k + 1) * KC // 2)
                dve.wait_ge(whi_ready, k + 1)
                dve.tensor_tensor(w_lo[:, part], w_raw[:, part], w_hi[:, part].bitcast(F32), ALU.subtract).then_inc(wlo_ready, 1)

            def finish(t, par):
                dve.wait_ge(rstd_ready, t + 1)
                wait_from(dve, stored[par], (t - par) * 8)
                dve.scalar_tensor_tensor(out=y[:, par], in0=out[:, par], scalar=rstd[:, par:par + 1], in1=gain[:],
                                         op0=ALU.mult, op1=ALU.mult).then_inc(y_ready, 1)

            def step(t, par):
                if not is_last(t):
                    low(t + 1, 1 - par)
                dve.wait_ge(acc_done, t + 1)
                dve.wait_ge(x_loaded[par], (t - par) * 8 + 16)
                wait_from(dve, y_ready, t - 1)
                dve.tensor_tensor(out[:, par], acc[:, par], x_in[:, par], ALU.add).then_inc(out_ready, 1)
                finish(t, par)

            each_tile(dve, step)

        @block.tensor
        def _(pe):
            pe.wait_ge(ident_ready, 1)

            def turn(t, par):
                pe.wait_ge(m_loaded[par], (t - par) * 8 + 16)
                wait_from(pe, lo_ready, t - 1)
                for k in range(KC):
                    mm = pe.transpose(t_ps[:, par, k], m_in[:, par, k * P:(k + 1) * P], ident[:])
                mm.then_inc(turned, 1)

            turn(0, 0)
            pe.wait_ge(wlo_ready, 2)

            def step(t, par):
                if not is_last(t):
                    turn(t + 1, 1 - par)
                pe.wait_ge(lo_ready, t + 1)
                wait_from(pe, out_ready, t - 1)
                for h in range(NH):
                    c = slice(h * BLK, (h + 1) * BLK)
                    terms = [(a, b, k) for k in range(KC) for a, b in ((h_hi, w_hi), (h_hi, w_lo), (h_lo, w_hi))]
                    for q, (a, b, k) in enumerate(terms):
                        mm = pe.matmul(acc[:, par, c], a[:, par, k], b[:, k, c], start=(q == 0), stop=(q == len(terms) - 1))
                mm.then_inc(acc_done, 1)

            each_tile(pe, step)


def build(nc, a, o):
    def scratch(name, shape):
        return nc.dram_tensor(name, shape, F32, kind="Internal").ap()

    z = scratch("z_scratch", [N_BLOCKS, ROWS, BLK])
    tail = scratch("tail_scratch", [ROWS, TAIL])
    logf = scratch("logf_scratch", [ROWS, HEADS])
    decay_key = scratch("decay_scratch", [2, P, PROMPT_TILES * HEADS])
    gla_cum = scratch("glacum_scratch", [B_HEADS // 2, P, ROWS])
    o_gla = scratch("ogla_scratch", [ROWS, D_B])
    decay_past = scratch("dpast_scratch", [DEC_BATCH * CHUNKS, 2 * HEADS, CHUNK_PAGES * PAGE])
    decay_new = scratch("dnew_scratch", [2 * HEADS, SAMPLE])
    y_a = scratch("ya_scratch", [ROWS, D_A])
    ext_prompt = scratch("extp_scratch", [CONV_W - 1 + SEQ, D_C])
    ext_sample = scratch("exts_scratch", [DEC_BATCH, CONV_W - 1 + DEC_SEQ, D_C])
    merged = scratch("merged_scratch", [ROWS, D_MODEL])
    project(nc, a["x_all"], a["g_norm"], a["w_main"], a["w_tail"], z, tail)
    forget_gates(nc, tail, a["b_forget"], logf, decay_key, o["logf_prompt"], o["logf_sample"])
    gla_decay(nc, tail, a["w_gla_up"], a["b_gla"], gla_cum)
    linear_attention(nc, z, gla_cum, a["state_gla"], o_gla, o["gla_prompt"], o["gla_sample"])
    attend_prompt(nc, z, decay_key, y_a)
    page_decay(nc, a["cache_logf"], a["page_table"], logf, decay_past, decay_new)
    attend_sample(nc, z, a["cache_k"], a["cache_v"], a["page_table"], decay_past, decay_new, y_a)
    conv_inputs(nc, z, a["state_conv"], ext_prompt, ext_sample, o["conv_prompt"], o["conv_sample"],
                o["k_prompt"], o["v_prompt"], o["k_sample"], o["v_sample"])
    merge_branches(nc, z, y_a, o_gla, ext_prompt, ext_sample, a["g_gla"], a["conv_w"],
                   [a["w_branch_a"], a["w_branch_b"], a["w_branch_c"]], merged)
    project_out(nc, a["x_all"], merged, a["w_out"], a["g_final"], o["y_prompt"], o["y_sample"])


def layout(inputs):
    import numpy as np
    a = {k: np.ascontiguousarray(v) for k, v in inputs.items()}
    x_all = np.zeros((ROWS, D_MODEL), a["x_prompt"].dtype)
    x_all[:SEQ] = a["x_prompt"][0]
    x_all[SEQ:SEQ + SAMPLE] = a["x_sample"].reshape(SAMPLE, D_MODEL)
    w = a["w_in"][0]
    forget = 3 * D_A
    low = forget + HEADS + D_A + 2 * D_BK + D_B
    main = np.ascontiguousarray(np.concatenate([w[:, :forget], w[:, forget + HEADS:low], w[:, low + LOW_RANK:]], axis=1))
    w_tail = np.ascontiguousarray(np.concatenate([w[:, forget:forget + HEADS], w[:, low:low + LOW_RANK]], axis=1))
    out = {k: v for k, v in a.items() if k not in ("x_prompt", "x_sample", "w_in")}
    out.update(x_all=x_all, w_main=main, w_tail=w_tail)
    return out


INPUTS = ("x_all", "w_main", "w_tail", "cache_k", "cache_v", "cache_logf", "state_gla", "state_conv", "page_table",
          "g_norm", "b_forget", "w_gla_up", "b_gla", "g_gla", "conv_w", "w_branch_a", "w_branch_b", "w_branch_c",
          "w_out", "g_final")
OUTPUTS = {
    "y_prompt": (1, SEQ, D_MODEL), "y_sample": (DEC_BATCH, DEC_SEQ, D_MODEL),
    "k_prompt": (1, 1, SEQ, HEADS, HEAD_DIM), "v_prompt": (1, 1, SEQ, HEADS, HEAD_DIM), "logf_prompt": (1, 1, SEQ, HEADS),
    "k_sample": (1, DEC_BATCH, DEC_SEQ, HEADS, HEAD_DIM), "v_sample": (1, DEC_BATCH, DEC_SEQ, HEADS, HEAD_DIM),
    "logf_sample": (1, DEC_BATCH, DEC_SEQ, HEADS),
    "gla_prompt": (1, 1, B_HEADS, B_KEY, B_VAL), "gla_sample": (1, DEC_BATCH, B_HEADS, B_KEY, B_VAL),
    "conv_prompt": (1, 1, CONV_W - 1, D_C), "conv_sample": (1, DEC_BATCH, CONV_W - 1, D_C),
}


def kernel(**inputs):
    import concourse.bacc as bacc
    from concourse.bass_utils import run_bass_kernel_spmd

    nc = bacc.Bacc("TRN2", target_bir_lowering=False, num_devices=1)
    arrays = layout(inputs)
    feeds = {f"in_{name}_dram": arrays[name] for name in INPUTS}
    a = {name: nc.dram_tensor(f"in_{name}_dram", arrays[name].shape, mybir.dt.from_np(arrays[name].dtype),
                              kind="ExternalInput").ap() for name in INPUTS}
    o = {name: nc.dram_tensor(f"out_{i}_dram", shape, F32, kind="ExternalOutput").ap()
         for i, (name, shape) in enumerate(OUTPUTS.items())}
    build(nc, a, o)
    results = run_bass_kernel_spmd(nc, [feeds], core_ids=[0]).results[0]
    return tuple(results[f"out_{i}_dram"] for i in range(len(OUTPUTS)))
```
